# Optimizing a Trainium2 kernel written in Bass

```python
import jax, jax.numpy as jnp
from jax import lax
import numpy as np
import math

D_MODEL = 1024
BATCH = 1
SEQ = 512
DEPTH = 1

N_RET_HEADS = 8
RET_HEAD_DIM = D_MODEL // N_RET_HEADS
RET_WIDTH = N_RET_HEADS * RET_HEAD_DIM
RET_CHUNK = 128
ROPE_BASE = 10000.0
CONV_WIDTH = D_MODEL
CONV_GROUPS = 8
CONV_K = 3
FFN_HIDDEN = -(-8 * D_MODEL // (3 * 256)) * 256
EPS = 1e-6
N_MOD = 6
IN_SPLITS = [RET_WIDTH, RET_WIDTH, RET_WIDTH, RET_WIDTH,
             CONV_WIDTH, CONV_WIDTH, CONV_WIDTH,
             D_MODEL, D_MODEL]
IN_COLS = sum(IN_SPLITS)


def rmsnorm(x, g):
    xf = x.astype(jnp.float32)
    y = xf * lax.rsqrt(jnp.mean(xf * xf, axis=-1, keepdims=True) + EPS)
    return (y * g.astype(jnp.float32)).astype(x.dtype)

def head_layernorm(y):
    yf = y.astype(jnp.float32)
    mu = jnp.mean(yf, axis=-1, keepdims=True)
    var = jnp.mean((yf - mu) ** 2, axis=-1, keepdims=True)
    return ((yf - mu) * lax.rsqrt(var + EPS)).astype(y.dtype)

def modulate(h, shift, scale):
    return h * (1.0 + scale[:, None, :]) + shift[:, None, :]

def rope(t, cos, sin):
    t1, t2 = jnp.split(t, 2, axis=-1)
    out = jnp.concatenate([t1 * cos - t2 * sin, t1 * sin + t2 * cos], axis=-1)
    return out.astype(t.dtype)

def retention_chunkwise(q, k, v, log_gamma):
    B, S, H, d = q.shape
    N = S // RET_CHUNK

    def to_chunks(t):
        return t.reshape(B, N, RET_CHUNK, H, t.shape[-1]).transpose(0, 3, 1, 2, 4)

    qc, kc, vc = to_chunks(q), to_chunks(k), to_chunks(v)
    idx = jnp.arange(RET_CHUNK, dtype=jnp.float32)
    rel = idx[:, None] - idx[None, :]
    lg = log_gamma[:, None, None]
    dmask = jnp.where(rel >= 0, jnp.exp(lg * jnp.maximum(rel, 0.0)), 0.0)
    scores = jnp.einsum('bhncd,bhnmd->bhncm', qc, kc) * dmask[None, :, None]
    inner = jnp.einsum('bhncm,bhnme->bhnce', scores, vc)
    zeta = jnp.exp(log_gamma[:, None] * (RET_CHUNK - 1 - idx)[None, :])
    kv = jnp.einsum('bhncd,bhnce->bhnde', kc * zeta[None, :, None, :, None], vc)
    chunk_decay = jnp.exp(log_gamma * RET_CHUNK)[None, :, None, None]

    def step(R, kv_n):
        return R * chunk_decay + kv_n, R

    _, R_prev = lax.scan(step, jnp.zeros_like(kv[:, :, 0]), kv.transpose(2, 0, 1, 3, 4))
    R_prev = R_prev.transpose(1, 2, 0, 3, 4)
    xi = jnp.exp(log_gamma[:, None] * (idx + 1.0)[None, :])
    cross = jnp.einsum('bhncd,bhnde->bhnce', qc, R_prev) * xi[None, :, None, :, None]
    out = inner + cross
    return out.transpose(0, 2, 3, 1, 4).reshape(B, S, H, vc.shape[-1])

def first_inputs(seed: int = 0) -> dict:
    key = jax.random.key(seed)
    ks = jax.random.split(key, 20)
    D = D_MODEL
    nrm = lambda k, shape, fan_in, s=1.0: s * jax.random.normal(k, shape, jnp.float32) * fan_in ** -0.5
    x = jax.random.normal(ks[0], (BATCH, SEQ, D), jnp.float32)
    c = jax.random.normal(ks[1], (BATCH, D), jnp.float32)
    positions = jnp.broadcast_to(jnp.arange(SEQ, dtype=jnp.int32)[None, :], (BATCH, SEQ))
    return {
        "x": x,
        "c": c,
        "positions": positions,
        "ada_w": nrm(ks[2], (DEPTH, D, N_MOD * D), D, 0.1),
        "ada_b": 0.02 * jax.random.normal(ks[3], (DEPTH, N_MOD * D), jnp.float32),
        "norm_mix_g": 1.0 + 0.02 * jax.random.normal(ks[4], (DEPTH, D), jnp.float32),
        "w_in": nrm(ks[5], (DEPTH, D, IN_COLS), D),
        "conv_w": nrm(ks[6], (DEPTH, CONV_K, CONV_WIDTH), CONV_K),
        "ret_w_out": nrm(ks[7], (DEPTH, RET_WIDTH, D), RET_WIDTH),
        "conv_w_out": nrm(ks[8], (DEPTH, CONV_WIDTH, D), CONV_WIDTH),
        "mix_w_out": nrm(ks[9], (DEPTH, D, D), D),
        "norm_ffn_g": 1.0 + 0.02 * jax.random.normal(ks[10], (DEPTH, D), jnp.float32),
        "ffn_w_gate": nrm(ks[11], (DEPTH, D, FFN_HIDDEN), D),
        "ffn_w_up": nrm(ks[12], (DEPTH, D, FFN_HIDDEN), D),
        "ffn_w_down": nrm(ks[13], (DEPTH, FFN_HIDDEN, D), FFN_HIDDEN),
        "final_norm_g": 1.0 + 0.02 * jax.random.normal(ks[14], (D,), jnp.float32),
    }

def first_block(x, c, positions, ada_w, ada_b, norm_mix_g, w_in, conv_w, ret_w_out,
              conv_w_out, mix_w_out, norm_ffn_g, ffn_w_gate, ffn_w_up, ffn_w_down,
              final_norm_g):
    B, S, D = x.shape
    H, d = N_RET_HEADS, RET_HEAD_DIM
    log_gamma = jnp.log(1.0 - 2.0 ** (-5.0 - jnp.arange(H, dtype=jnp.float32)))
    inv_freq = 1.0 / (ROPE_BASE ** (jnp.arange(0, d, 2, dtype=jnp.float32) / d))
    ang = positions.astype(jnp.float32)[..., None] * inv_freq
    cos, sin = jnp.cos(ang)[:, :, None, :], jnp.sin(ang)[:, :, None, :]
    split_pts = list(np.cumsum(IN_SPLITS)[:-1])
    cs = jax.nn.silu(c)

    for l in range(DEPTH):
        mod = cs @ ada_w[l] + ada_b[l]
        sh_m, sc_m, gt_m, sh_f, sc_f, gt_f = jnp.split(mod, N_MOD, axis=-1)

        h = modulate(rmsnorm(x, norm_mix_g[l]), sh_m, sc_m)
        proj = h @ w_in[l]
        q, k, v, g_ret, b_cv, c_cv, u_cv, g_a, g_b = jnp.split(proj, split_pts, axis=-1)

        q = rope(q.reshape(B, S, H, d), cos, sin)
        k = rope(k.reshape(B, S, H, d), cos, sin) * (d ** -0.5)
        v = v.reshape(B, S, H, d)
        y_ret = head_layernorm(retention_chunkwise(q, k, v, log_gamma)).reshape(B, S, RET_WIDTH)
        y_a = (jax.nn.silu(g_ret) * y_ret) @ ret_w_out[l]

        u = c_cv * u_cv
        u_pad = jnp.pad(u, ((0, 0), (CONV_K - 1, 0), (0, 0)))
        w = conv_w[l]
        conv = u_pad[:, 0:S] * w[0]
        for tap in range(1, CONV_K):
            conv = conv + u_pad[:, tap:tap + S] * w[tap]
        y_b = (b_cv * conv) @ conv_w_out[l]

        merged = jax.nn.sigmoid(g_a) * y_a + jax.nn.sigmoid(g_b) * y_b
        x = x + gt_m[:, None, :] * (merged @ mix_w_out[l])

        h = modulate(rmsnorm(x, norm_ffn_g[l]), sh_f, sc_f)
        f = (jax.nn.silu(h @ ffn_w_gate[l]) * (h @ ffn_w_up[l])) @ ffn_w_down[l]
        x = x + gt_f[:, None, :] * f

    return rmsnorm(x, final_norm_g)


N_DIFF_HEADS = 4
DIFF_HEAD_DIM = 64
DIFF_V_DIM = 2 * DIFF_HEAD_DIM
DIFF_WIDTH = N_DIFF_HEADS * DIFF_V_DIM
N_MLSTM_HEADS = 4
MLSTM_QK_DIM = 64
MLSTM_V_DIM = 128
MLSTM_WIDTH = N_MLSTM_HEADS * MLSTM_V_DIM
MIX_WIDTH = DIFF_WIDTH + MLSTM_WIDTH
CONV_WIDTH_2 = 4
CHUNK = 64
Q_BLOCK = 128
D_FF = 4 * D_MODEL
ROPE_THETA = 10000.0

IN_SIZES = (
    N_DIFF_HEADS * 2 * DIFF_HEAD_DIM,
    N_DIFF_HEADS * 2 * DIFF_HEAD_DIM,
    DIFF_WIDTH,
    N_MLSTM_HEADS * MLSTM_QK_DIM,
    N_MLSTM_HEADS * MLSTM_QK_DIM,
    MLSTM_WIDTH,
    MLSTM_WIDTH,
    N_MLSTM_HEADS,
    N_MLSTM_HEADS,
)
IN_WIDTH = sum(IN_SIZES)
IN_OFFSETS = tuple(int(o) for o in np.cumsum(IN_SIZES)[:-1])
CONV_CH = 2 * N_MLSTM_HEADS * MLSTM_QK_DIM


def lambda_init(layer):
    return 0.8 - 0.6 * math.exp(-0.3 * layer)

def rmsnorm_2(x, g):
    xf = x.astype(jnp.float32)
    y = xf * lax.rsqrt(jnp.mean(xf * xf, axis=-1, keepdims=True) + EPS)
    return (y * g.astype(jnp.float32)).astype(x.dtype)

def rope_2(x, pos):
    d = x.shape[-1]
    inv = ROPE_THETA ** (-jnp.arange(0, d, 2, dtype=jnp.float32) / d)
    ang = pos.astype(jnp.float32)[:, None] * inv[None, :]
    cos = jnp.cos(ang)[None, :, None, :]
    sin = jnp.sin(ang)[None, :, None, :]
    xf = x.astype(jnp.float32)
    x1, x2 = xf[..., : d // 2], xf[..., d // 2:]
    out = jnp.concatenate([x1 * cos - x2 * sin, x2 * cos + x1 * sin], axis=-1)
    return out.astype(x.dtype)

def diff_attention(q, k, v, lam):
    S = q.shape[3]
    scale = DIFF_HEAD_DIM ** -0.5
    outs = []
    for blk in range(S // Q_BLOCK):
        lo, hi = blk * Q_BLOCK, (blk + 1) * Q_BLOCK
        qb = q[:, :, :, lo:hi]
        kb = k[:, :, :, :hi]
        s = jnp.einsum('bhcqd,bhckd->bhcqk', qb, kb).astype(jnp.float32) * scale
        mask = (lo + jnp.arange(Q_BLOCK))[:, None] >= jnp.arange(hi)[None, :]
        s = jnp.where(mask, s, -jnp.inf)
        p = jax.nn.softmax(s, axis=-1)
        p_diff = p[:, :, 0] - lam * p[:, :, 1]
        outs.append(jnp.einsum('bhqk,bhkv->bhqv', p_diff.astype(v.dtype), v[:, :, :hi]))
    return jnp.concatenate(outs, axis=2)

def mlstm_chunkwise(q, k, v, i_pre, logf):
    B, H, S, dqk = q.shape
    dv = v.shape[-1]
    nc = S // CHUNK
    q = q * (dqk ** -0.5)

    def chunked(t):
        t = t.reshape(t.shape[:2] + (nc, CHUNK) + t.shape[3:])
        return jnp.moveaxis(t, 2, 0)

    xs = (chunked(q), chunked(k), chunked(v), chunked(i_pre), chunked(logf))
    causal = jnp.tril(jnp.ones((CHUNK, CHUNK), dtype=bool))

    def step(carry, inp):
        C, n, m = carry
        qc, kc, vc, ic, fc = inp
        b = jnp.cumsum(fc, axis=-1)
        g = b[..., -1]
        logD = b[..., :, None] - b[..., None, :] + ic[..., None, :]
        logD = jnp.where(causal, logD, -jnp.inf)
        inter = b + m[..., None]
        m_comb = jnp.maximum(inter, jnp.max(logD, axis=-1))
        scores = jnp.einsum('bhjd,bhsd->bhjs', qc, kc) * jnp.exp(logD - m_comb[..., None])
        w_inter = jnp.exp(inter - m_comb)
        num = (w_inter[..., None] * jnp.einsum('bhjd,bhdv->bhjv', qc, C)
               + jnp.einsum('bhjs,bhsv->bhjv', scores, vc))
        den = w_inter * jnp.einsum('bhjd,bhd->bhj', qc, n) + jnp.sum(scores, axis=-1)
        h = num / jnp.maximum(jnp.abs(den), jnp.exp(-m_comb))[..., None]
        log_w = g[..., None] - b + ic
        m_new = jnp.maximum(g + m, jnp.max(log_w, axis=-1))
        decay = jnp.exp(g + m - m_new)
        w = jnp.exp(log_w - m_new[..., None])
        C_new = decay[..., None, None] * C + jnp.einsum('bhs,bhsd,bhsv->bhdv', w, kc, vc)
        n_new = decay[..., None] * n + jnp.einsum('bhs,bhsd->bhd', w, kc)
        return (C_new, n_new, m_new), h

    init = (jnp.zeros((B, H, dqk, dv), jnp.float32),
            jnp.zeros((B, H, dqk), jnp.float32),
            jnp.zeros((B, H), jnp.float32))
    _, hs = lax.scan(step, init, xs)
    return jnp.moveaxis(hs, 0, 2).reshape(B, H, S, dv)

def causal_dwconv(x, w, b):
    S = x.shape[1]
    xp = jnp.pad(x, ((0, 0), (CONV_WIDTH_2 - 1, 0), (0, 0)))
    y = b
    for j in range(CONV_WIDTH_2):
        y = y + w[j] * xp[:, j:j + S]
    return y

def second_inputs(seed: int = 0) -> dict:
    key = jax.random.key(seed)
    ks = jax.random.split(key, 20)
    f32 = jnp.float32
    nrm = lambda k, shape, s: jax.random.normal(k, shape, f32) * s
    gain = lambda k, shape: 1.0 + 0.05 * jax.random.normal(k, shape, f32)
    return {
        "x": jax.random.normal(ks[0], (BATCH, SEQ, D_MODEL), f32),
        "norm_mix_pre": gain(ks[1], (DEPTH, D_MODEL)),
        "w_in": nrm(ks[2], (DEPTH, D_MODEL, IN_WIDTH), D_MODEL ** -0.5),
        "conv_w": nrm(ks[3], (DEPTH, CONV_WIDTH_2, CONV_CH), CONV_WIDTH_2 ** -0.5),
        "conv_b": nrm(ks[4], (DEPTH, CONV_CH), 0.01),
        "b_igate": nrm(ks[5], (DEPTH, N_MLSTM_HEADS), 0.1),
        "b_fgate": 3.0 + nrm(ks[6], (DEPTH, N_MLSTM_HEADS), 0.5),
        "lambda_q1": nrm(ks[7], (DEPTH, DIFF_HEAD_DIM), 0.1),
        "lambda_k1": nrm(ks[8], (DEPTH, DIFF_HEAD_DIM), 0.1),
        "lambda_q2": nrm(ks[9], (DEPTH, DIFF_HEAD_DIM), 0.1),
        "lambda_k2": nrm(ks[10], (DEPTH, DIFF_HEAD_DIM), 0.1),
        "diff_norm": gain(ks[11], (DEPTH, DIFF_V_DIM)),
        "mlstm_norm": gain(ks[12], (DEPTH, N_MLSTM_HEADS, MLSTM_V_DIM)),
        "w_out": nrm(ks[13], (DEPTH, MIX_WIDTH, D_MODEL), MIX_WIDTH ** -0.5),
        "norm_mix_post": gain(ks[14], (DEPTH, D_MODEL)),
        "norm_mlp_pre": gain(ks[15], (DEPTH, D_MODEL)),
        "w_up": nrm(ks[16], (DEPTH, D_MODEL, D_FF), D_MODEL ** -0.5),
        "w_down": nrm(ks[17], (DEPTH, D_FF, D_MODEL), D_FF ** -0.5),
        "norm_mlp_post": gain(ks[18], (DEPTH, D_MODEL)),
    }

def second_block(x, norm_mix_pre, w_in, conv_w, conv_b, b_igate, b_fgate,
              lambda_q1, lambda_k1, lambda_q2, lambda_k2, diff_norm, mlstm_norm,
              w_out, norm_mix_post, norm_mlp_pre, w_up, w_down, norm_mlp_post):
    B, S, _ = x.shape
    pos = jnp.arange(S, dtype=jnp.int32)
    for l in range(DEPTH):
        lam_init = lambda_init(l)
        h = rmsnorm_2(x, norm_mix_pre[l])
        proj = h @ w_in[l]
        dq, dk, dvv, mq, mk, mv, mo, mi, mf = jnp.split(proj, IN_OFFSETS, axis=-1)

        dq = rope_2(dq.reshape(B, S, 2 * N_DIFF_HEADS, DIFF_HEAD_DIM), pos)
        dk = rope_2(dk.reshape(B, S, 2 * N_DIFF_HEADS, DIFF_HEAD_DIM), pos)
        dq = dq.reshape(B, S, N_DIFF_HEADS, 2, DIFF_HEAD_DIM).transpose(0, 2, 3, 1, 4)
        dk = dk.reshape(B, S, N_DIFF_HEADS, 2, DIFF_HEAD_DIM).transpose(0, 2, 3, 1, 4)
        dvv = dvv.reshape(B, S, N_DIFF_HEADS, DIFF_V_DIM).transpose(0, 2, 1, 3)
        lam = (jnp.exp(jnp.sum(lambda_q1[l].astype(jnp.float32) * lambda_k1[l].astype(jnp.float32)))
               - jnp.exp(jnp.sum(lambda_q2[l].astype(jnp.float32) * lambda_k2[l].astype(jnp.float32)))
               + lam_init)
        o_diff = diff_attention(dq, dk, dvv, lam)
        o_diff = rmsnorm_2(o_diff, diff_norm[l]) * (1.0 - lam_init)
        o_diff = o_diff.transpose(0, 2, 1, 3).reshape(B, S, DIFF_WIDTH)

        qk = causal_dwconv(jnp.concatenate([mq, mk], axis=-1), conv_w[l], conv_b[l])
        qk = jax.nn.silu(qk)
        mq, mk = qk[..., :CONV_CH // 2], qk[..., CONV_CH // 2:]
        to_heads = lambda t, d: t.reshape(B, S, N_MLSTM_HEADS, d).transpose(0, 2, 1, 3).astype(jnp.float32)
        i_pre = (mi + b_igate[l]).astype(jnp.float32).transpose(0, 2, 1)
        logf = jax.nn.log_sigmoid((mf + b_fgate[l]).astype(jnp.float32)).transpose(0, 2, 1)
        hm = mlstm_chunkwise(to_heads(mq, MLSTM_QK_DIM), to_heads(mk, MLSTM_QK_DIM),
                             to_heads(mv, MLSTM_V_DIM), i_pre, logf)
        hm = rmsnorm_2(hm.transpose(0, 2, 1, 3), mlstm_norm[l]).astype(x.dtype)
        o_mlstm = hm.reshape(B, S, MLSTM_WIDTH) * jax.nn.sigmoid(mo)

        mixed = jnp.concatenate([o_diff.astype(x.dtype), o_mlstm], axis=-1) @ w_out[l]
        x = x + rmsnorm_2(mixed, norm_mix_post[l])

        h = rmsnorm_2(x, norm_mlp_pre[l])
        u = jnp.square(jax.nn.relu(h @ w_up[l]))
        x = x + rmsnorm_2(u @ w_down[l], norm_mlp_post[l])
    return x


def setup_inputs(seed=0):
    out = dict(first_inputs(seed))
    for name, value in second_inputs(seed + 1).items():
        if name != "x":
            out[name + "_2"] = value
    return out


def reference(
    x, c, positions, ada_w, ada_b, norm_mix_g, w_in, conv_w, ret_w_out, conv_w_out, mix_w_out,
    norm_ffn_g, ffn_w_gate, ffn_w_up, ffn_w_down, final_norm_g, norm_mix_pre_2, w_in_2,
    conv_w_2, conv_b_2, b_igate_2, b_fgate_2, lambda_q1_2, lambda_k1_2, lambda_q2_2,
    lambda_k2_2, diff_norm_2, mlstm_norm_2, w_out_2, norm_mix_post_2, norm_mlp_pre_2, w_up_2,
    w_down_2, norm_mlp_post_2,
):
    x = first_block(
        x, c, positions, ada_w, ada_b, norm_mix_g, w_in, conv_w, ret_w_out, conv_w_out,
        mix_w_out, norm_ffn_g, ffn_w_gate, ffn_w_up, ffn_w_down, final_norm_g,
    )
    return second_block(
        x, norm_mix_pre_2, w_in_2, conv_w_2, conv_b_2, b_igate_2, b_fgate_2, lambda_q1_2,
        lambda_k1_2, lambda_q2_2, lambda_k2_2, diff_norm_2, mlstm_norm_2, w_out_2,
        norm_mix_post_2, norm_mlp_pre_2, w_up_2, w_down_2, norm_mlp_post_2,
    )


_drawn_inputs = setup_inputs


def setup_inputs(seed=0):
    import zlib

    import numpy as np

    out = dict(_drawn_inputs(seed))
    spreads = {}
    factors = {'norm_mix_g': 8.0,
     'norm_ffn_g': 64.0,
     'conv_b_2': 8.0,
     'b_igate_2': 64.0,
     'lambda_k2_2': 6.128,
     'ret_w_out': 3.312}
    for name, (base, spread) in spreads.items():
        noise = np.random.default_rng([zlib.crc32(name.encode()), seed]).standard_normal(out[name].shape)
        drawn = base * np.exp(spread * noise) if base else spread * noise
        out[name] = __import__('jax').numpy.asarray(drawn.astype(out[name].dtype))
    for name, factor in factors.items():
        out[name] = (out[name] * factor).astype(out[name].dtype)
    return out
```

```python
from contextlib import ExitStack

import numpy as np

import concourse.bass as bass
from concourse import mybir

F32 = mybir.dt.float32
F32R = mybir.dt.float32r
ALU = mybir.AluOpType
ACT = mybir.ActivationFunctionType
AX = mybir.AxisListType

P = 128
D = 1024
S = 512
KC = D // P
NB = S // P
UC = 256
BUFS = 2
EPS = 1e-6
HEAD = 128
DQK = 64
BIG = 1e30
TRI = [512, 384, 256, 128]
TRI_AT = [0, 512, 896, 1152]

U_CONV = 0
U_COUT = 12
U_RET = 20
U_GA = 36
U_ROUT = 40
U_MIX = 44
U_FFN = 48
U_IN2 = 82
IN2 = ("mq", "mk", "gates", "mv0", "mv1", "mo0", "mo1", "dq0", "dk0", "dv0", "dq1", "dk1", "dv1")
IN2_COL = {"dq0": 0, "dq1": 256, "dk0": 512, "dk1": 768, "dv0": 1024, "dv1": 1280, "mq": 1536, "mk": 1792,
           "mv0": 2048, "mv1": 2304, "mo0": 2560, "mo1": 2816}
U_OUT2 = 95
U_MLP = 99
U_END = 131

X_H1, X_CV, X_RET, X_MRG, X_H2, X_HID, X_H3, X_O, X_H4, X_HID2 = 0, 4, 8, 12, 16, 20, 31, 35, 43, 47

C_ID, C_MS, C_MQ, C_COS2, C_SIN2, C_INVF = 0, 128, 256, 384, 896, 1408
C_ALL = C_INVF + 1

PAR1 = {"ada_b": (0, 48), "norm_mix_g": (48, 8), "norm_ffn_g": (56, 8), "final_norm_g": (64, 8),
        "conv_w": (72, 24), "c": (96, 8)}
PAR2 = {"norm_mix_pre_2": (0, 8), "norm_mix_post_2": (8, 8), "norm_mlp_pre_2": (16, 8),
        "norm_mlp_post_2": (24, 8), "conv_w_2": (32, 16), "conv_b_2": (48, 4), "diff_norm_2": (52, 1),
        "mlstm_norm_2": (53, 4)}
N1, N2 = 104, 57

Z_ALL = 9232
QAT = [0, 128, 384, 768]
LAMBDA_INIT = 0.2


def done(u):
    return u + 1 + BUFS


def free(u):
    return u + 1


class Steps:

    def __init__(self, eng, sem):
        self.eng, self.sem, self.n, self.at = eng, sem, 0, 0

    def link(self, ins):
        self.n += 1
        ins.then_inc(self.sem, 1)
        self.eng.wait_ge(self.sem, self.at + self.n)

    def loop(self, start, end, per):
        return _StepLoop(self, start, end, per)


class _StepLoop:
    def __init__(self, steps, start, end, per):
        self.s, self.start, self.end, self.per = steps, start, end, per
        self.ctx = ExitStack()

    def __enter__(self):
        i = self.ctx.enter_context(self.s.eng.Fori(self.start, self.end))
        self.was, self.n0 = self.s.at, self.s.n
        self.s.at = self.was + (i - self.start) * self.per if self.start else self.was + i * self.per
        return i

    def __exit__(self, *e):
        r = self.ctx.__exit__(*e)
        if e[0] is None:
            assert self.s.n - self.n0 == self.per, (self.s.n - self.n0, self.per)
            self.s.at = self.was
            self.s.n = self.n0 + self.per * (self.end - self.start)
        return r


def program(nc, t_in, out):
    ctx = ExitStack()
    with ctx:
        def sb(name, shape, dt=F32, c=ctx):
            return c.enter_context(nc.sbuf_tensor(name, shape, dt))

        X = sb("x_res", [P, KC, S])
        raw = sb("w_raw", [P, BUFS, KC, UC])
        w_hi = sb("w_hi", [P, BUFS, KC, UC], F32R)
        w_lo = sb("w_lo", [P, BUFS, KC, UC], F32R)
        ga_hi = sb("ga_hi", [P, KC, S], F32R)
        ga_lo = sb("ga_lo", [P, KC, S], F32R)
        acc = sb("acc", [P, KC, S])
        con = sb("con", [P, C_ALL])
        col1 = sb("col1", [P, N1])
        col2 = sb("col2", [P, N2])
        cs = sb("cs", [P, KC])
        mod = sb("mod", [P, 48])
        gs = sb("gs", [P, 16])
        small = sb("small", [P, 64])
        ones = sb("ones", [P, P])
        par2 = sb("par2", [P, 4 * P])
        sqp = sb("sqp", [P, 2, S])
        rstd = sb("rstd", [P, S])
        tmp = sb("tmp", [P, 2, S])
        rope1 = sb("rope1", [P, 2, S])
        em2 = sb("em2", [P, S])
        pm_2 = sb("pm_2", [P, TRI[2]])
        Z = sb("work", [P, Z_ALL])
        with ExitStack() as top:
            h_hi = sb("h_hi", [P, KC, S], F32R, top)
            h_lo = sb("h_lo", [P, KC, S], F32R, top)
        with ExitStack() as top:
            att = sb("att", [P, 8192], F32, top)
        h2_hi = sb("h2_hi", [P, KC, S], F32R)
        h2_lo = sb("h2_lo", [P, KC, S], F32R)

        G = ctx.enter_context(nc.psum_tensor("gemm_ps", [P, 4, S], F32))
        T = ctx.enter_context(nc.psum_tensor("tail_ps", [P, 4, S], F32))
        sems = {}

        def sm(name):
            if name not in sems:
                sems[name] = ctx.enter_context(nc.semaphore(name))
            return sems[name]

        ident = con[:, C_ID:C_ID + P]
        mask_s, mask_q = con[:, C_MS:C_MS + P], con[:, C_MQ:C_MQ + P]
        cos2, sin2 = con[:, C_COS2:C_COS2 + S], con[:, C_SIN2:C_SIN2 + S]
        xin = acc[:, :, :].rearrange("p a b -> p (a b)").rearrange("p (b d) -> p b d", b=NB)
        prow1, prow2 = sqp[0:N1, 0, 0:P], par2[0:N2, 0:P]
        lam_row = small[0:1, 0:8]

        def zv(a, n, w):
            return Z[:, a:a + n * w].rearrange("p (n w) -> p n w", n=n)

        u_cv, cv = zv(0, 2, S), zv(2052, 2, S)
        u_pad = Z[:, 1024:1024 + 2 * 514].rearrange("p (n w) -> p n w", n=2)
        ada = zv(3076, 2, 2048)
        ada_sum = Z[:, 7172:7172 + 2048]
        FIRST_SLOTS = 6

        def ada_first(t):
            k = t % FIRST_SLOTS
            return att[:, 2048 * k:2048 * (k + 1)] if k < 4 else ada[:, k - 4]

        qq, kk, sw, gg = zv(0, 2, S), zv(1024, 2, S), zv(3072, 2, S), zv(4096, 2, S)
        vv = zv(2048, NB, UC)
        decay = zv(5120, 2, S)
        pp = [Z[:, 6144 + 1280 * h:6144 + 1280 * (h + 1)] for h in range(2)]
        v_mean = small[:, 8:16]
        pp_blocks = [[q[:, TRI_AT[b]:TRI_AT[b] + TRI[b]] for b in range(NB)] for q in pp]
        sga = zv(0, KC, S)
        xg = zv(4096, KC, S)
        gate = zv(0, 2, S)
        q2, k2 = zv(0, 4, S), zv(2048, 4, S)
        mqk = [zv(4096, 2, S), zv(5120, 2, S)]
        mo = zv(6144, 4, S)
        m_pad = Z[:, 8192:8192 + 2 * 515].rearrange("p (n w) -> p n w", n=2)
        vd, vm = [acc[:, 4 * i:4 * i + 4, :] for i in range(2)]
        out_tok = Z[:, 0:NB * D].rearrange("p (b d) -> p b d", b=NB)
        small_rope = sqp[:, 1]
        xr = acc
        pr = [[att[:, 1280 * (2 * k + c):1280 * (2 * k + c + 1)] for c in range(2)] for k in range(2)]
        pt, dsq, drs = att[:, 5120:6400], att[:, 6400:6400 + S], att[:, 6400 + S:6400 + 2 * S]
        sums = [small[:, 40:48], small[:, 8:16]]
        nmax = [small[:, 48:56], small[:, 16:24]]
        row_top = small[:, 56:60]
        r12_col = small[:, 60:64]
        pm = [rope1[:, 0], rope1[:, 1, 0:TRI[1]], pm_2[:, :], rope1[:, 1, TRI[1]:S]]
        nm, nmd = [Z[:, 8192 + S * k:8192 + S * (k + 1)] for k in range(2)]
        i_row, f_row, f_row2, lf_row, b_row, m_row, one_row, zero_row = [Z[0:4, S * k:S * (k + 1)] for k in range(8)]
        nm_row, bm_row = par2[0:4, 0:S], tmp[0:4, 1]
        gain12 = small[:, 24:32]
        a_col, nlam, dgain = small[:, 16:32], small[:, 34:35], small[:, 35:36]

        def sel(h):
            return ident[0:4, h:h + 1].to_broadcast([4, P])

        spare = Z[:, Z_ALL - 2 * S:Z_ALL].rearrange("p (n w) -> p n w", n=2)
        norm_tmp = [tmp[:, :, :], u_cv]
        pool_tmp = zv(4096, 2, S)
        sq_sum = [rope1[:, 0], rope1[:, 1]]
        POOL_SQ = {k: (1, k in (4, 16, 20, 24)) for k in (4, 5, 6, 16, 17, 18, 20, 21, 22, 24, 25, 26)}
        POOL_SQ.update({k: (k % 2, k < 10) for k in range(8, 14)})
        POOL_SQ = {k: POOL_SQ[k] for k in sorted(POOL_SQ)}

        def bc2(ap):
            return ap.unsqueeze(1).to_broadcast([P, 2, S])

        def ps(p):
            return G[:, 2 * p:2 * p + 2, :]

        def sq_buf(k):
            return sqp[:, :, :] if k % 2 == 0 else (u_cv if k < 4 else spare)

        def w(name):
            return t_in[name][0].rearrange("(t p) n -> p t n", p=P)

        S_BANK = [(0, 0), (1, 0), (2, 0), (1, 384)]
        Q_BANK = [(1, 384), (2, 0), (1, 0), (0, 0)]

        def turned(h, b):
            q, at = S_BANK[b]
            if h == 3:
                return T[:, q, at:at + TRI[b]]
            return (T[:, 3, 0:S], G[:, 3, 0:TRI[1]], T[:, 3, 0:TRI[2]], G[:, 3, TRI[1]:S])[b]

        def pv_bank(h):
            return G[:, 3] if h < 3 else T[:, 3]

        def var_bank(h):
            return T[:, 3] if h < 3 else T[:, 0]

        block = ctx.enter_context(nc.Block())

        @block.sync
        def _(sp):
            def at(n):
                return n if isinstance(n, int) else sp.snap(n)

            def load(u, p, src, kc=KC):
                sp.wait_ge(sm("lo_split"), free(u))
                sp.sem_inc(sm("loads"), 1)
                sp.dma_start(raw[:, p, 0:kc], src).then_inc(sm(f"raw_in{p}"), 16)

            def pair(name, n):
                return w(name)[:, :, bass.ds(at(n), UC)]

            n = 0
            for name, (a, k) in PAR1.items():
                src = t_in[name]
                if name == "final_norm_g":
                    src = src.rearrange("(a n) -> a n", a=1)
                if name == "conv_w":
                    src = src[0]
                sp.dma_start(sqp[a:a + k, 0, 0:P], src.rearrange("a (k p) -> (a k) p", p=P)).then_inc(sm("par_in"), 16)
                n += 16
            sp.dma_start(con[:, 0:P], t_in["consts"][:, 0:P]).then_inc(sm("par_in"), 16)

            def load_ada_first(t):
                if t >= FIRST_SLOTS:
                    sp.wait_ge(sm("ada_used"), done(t - FIRST_SLOTS))
                sp.dma_start(ada_first(t), t_in["ada_w"][0][t * P:(t + 1) * P, 0:2048])\
                    .then_inc(sm(f"ada_first{t % FIRST_SLOTS}"), 16)

            def load_ada(a, p, third, t):
                src = t_in["ada_w"][0][bass.ds(at(t * P), P), third * 2048:(third + 1) * 2048]
                sp.wait_ge(sm("ada_used"), free(a))
                sp.sem_inc(sm("loads"), 1)
                sp.dma_start(ada[:, p], src).then_inc(sm(f"ada_in{p}"), 16)

            sp.dma_start(xin, t_in["x"][0].rearrange("(b p) d -> p b d", p=P)).then_inc(sm("x_in"), 16)
            for t in range(FIRST_SLOTS):
                load_ada_first(t)
            for name, (a, k) in PAR2.items():
                src = t_in[name]
                if name in ("conv_w_2", "mlstm_norm_2"):
                    src = src[0]
                sp.dma_start(par2[a:a + k, 0:P], src.rearrange("a (k p) -> (a k) p", p=P)).then_inc(sm("par2_in"), 16)
            sp.dma_start(small[0:4, 32:33], t_in["b_igate_2"].rearrange("a n -> n a")).then_inc(sm("par2_in"), 16)
            sp.dma_start(small[0:4, 33:34], t_in["b_fgate_2"].rearrange("a n -> n a")).then_inc(sm("par2_in"), 16)
            for i, name in enumerate(("lambda_q1_2", "lambda_k1_2", "lambda_q2_2", "lambda_k2_2")):
                sp.dma_start(par2[0:1, P + 64 * i:P + 64 * i + 64], t_in[name]).then_inc(sm("par2_in"), 16)
            for t in range(FIRST_SLOTS, KC):
                load_ada_first(t)
            load(U_CONV, 0, pair("w_in", 6144))
            sp.dma_start(con[:, P:C_ALL], t_in["consts"][:, P:C_ALL]).then_inc(sm("con_in"), 16)
            sp.dma_start(rope1[:, 1].bitcast(mybir.dt.int32),
                         t_in["positions"][0:1, :].to_broadcast([P, S])).then_inc(sm("pos_in"), 16)
            with sp.Fori(0, 2) as i:
                for k in range(6):
                    if k < 5:
                        col = (6144, 5120, 4096)[(k + 1) % 3] + (k + 1) // 3 * UC
                        load(U_CONV + 6 * i + k + 1, (k + 1) % 2, pair("w_in", col + i * 2 * UC))
                    else:
                        load(U_CONV + 6 * i + 6, 0, pair("w_in", 6144 + 2 * UC + i * (8192 - 6144 - 2 * UC)))
                    if k < 4:
                        load_ada(8 + 4 * i + k, k % 2, 1, 4 * i + k)
            with sp.Fori(0, 3) as i:
                load_ada(16 + 2 * i, 0, 2, 2 * i)
                load(U_COUT + 2 * i + 1, 1, pair("conv_w_out", i * UC))
                load_ada(17 + 2 * i, 1, 2, 2 * i + 1)
                load(U_COUT + 2 * i + 2, 0, pair("w_in", 8192 + UC + i * UC))
            load_ada(22, 0, 2, 6)
            load(U_COUT + 7, 1, pair("conv_w_out", 3 * UC))
            load_ada(23, 1, 2, 7)
            dec = t_in["decay"]
            with sp.Fori(0, 4) as i:
                for m in range(4):
                    load(U_RET + 4 * i + m, m % 2, pair("w_in", m * D + i * UC))
                    if m == 0:
                        src = dec[bass.ds(at(2 * i), 2)].rearrange("h p s -> p h s")
                        sp.wait_ge(sm("scores_used"), 2 * i + 2)
                        sp.sem_inc(sm("loads"), 1)
                        sp.wait_ge(sm("ada_used"), done(23))
                        sp.dma_start(decay, src)\
                            .then_inc(sm("decay_in"), 16)
            for ph, name, col in ((U_GA, "w_in", 7168), (U_ROUT, "ret_w_out", 0), (U_MIX, "mix_w_out", 0)):
                with sp.Fori(0, 2) as i:
                    for m in range(2):
                        load(ph + 2 * i + m, m, pair(name, col + (2 * i + m) * UC))

            def ffn_loads(u, base, pairs, kc):
                with sp.Fori(0, pairs) as i:
                    load(u + 2 * i, 0, pair("ffn_w_gate", base * P + i * UC))
                    load(u + 2 * i + 1, 1, pair("ffn_w_up", base * P + i * UC))
                with sp.Fori(0, 2) as i:
                    for m in range(2):
                        src = t_in["ffn_w_down"][0][bass.ds(at(base * P), kc * P), bass.ds(at(i * 2 * UC + m * UC), UC)]
                        load(u + 2 * pairs + 2 * i + m, m, src.rearrange("(t p) n -> p t n", p=P), kc)

            with sp.Fori(0, 2) as g:
                ffn_loads(U_FFN + 12 * g, g * 8, 4, 8)
            ffn_loads(U_FFN + 24, 16, 3, 6)

            for k, kind in enumerate(IN2):
                u = U_IN2 + k
                if kind == "gates":
                    sp.wait_ge(sm("lo_split"), free(u))
                    src = w("w_in_2")[:, :, 3072:3080].rearrange("p t (g c) -> p t g c", g=2)
                    for g in range(2):
                        sp.dma_start(raw[:, u % 2, :, 32 * g:32 * g + 4], src[:, :, g, :])\
                            .then_inc(sm("gate_w_in" if g else f"raw_in{u % 2}"), 16)
                else:
                    load(u, u % 2, pair("w_in_2", IN2_COL[kind]))
            for m in range(4):
                load(U_OUT2 + m, (U_OUT2 + m) % 2, pair("w_out_2", m * UC))
            with sp.Fori(0, 4) as g:
                for m in range(8):
                    u = U_MLP + 8 * g + m
                    p = (U_MLP + m) % 2
                    if m < 4:
                        load(u, p, pair("w_up_2", g * D + m * UC))
                    else:
                        src = t_in["w_down_2"][0][bass.ds(at(g * D), D), (m - 4) * UC:(m - 3) * UC]
                        load(u, p, src.rearrange("(t p) n -> p t n", p=P))
            ov = out[0].rearrange("(b p) d -> p b d", p=P)
            for j in range(4):
                sp.wait_ge(sm("out_ready"), j + 1)
                sp.dma_start(ov[:, :, j * UC:(j + 1) * UC], out_tok[:, :, j * UC:(j + 1) * UC])\
                    .then_inc(sm("out_sent"), 16)
            sp.wait_ge(sm("out_sent"), 64)

        @block.gpsimd
        def _(pool):
            TWO_PI = 2 * np.pi
            parts, rest = [], TWO_PI
            for k in range(3):
                q = 2.0 ** (np.floor(np.log2(rest)) - 7)
                parts.append(float(np.floor(rest / q) * q))
                rest -= parts[-1]
            parts.append(float(np.float32(rest)))
            ROUND = 1.5 * 2.0 ** 23
            step = Steps(pool, sm("pool_step"))
            step.link(pool.memset(u_pad[:, :, 0:2], 0.0))
            step.link(pool.memset(ones[:, :], 1.0))
            pool.sem_inc(sm("pads"), 1)
            pool.wait_ge(sm("rstd_ready"), 1)
            pool.wait_ge(sm("x_ready"), 8)
            for j in range(4):
                pool.tensor_tensor(xr[:, 2 * j:2 * j + 2], X[:, 2 * j:2 * j + 2], bc2(rstd[:, :]), ALU.mult)\
                    .then_inc(sm("xr_ready"), 1)
            ang, n, prod = rope1[:, 0], rope1[:, 1], small_rope
            pool.wait_ge(sm("pos_in"), 16)
            pool.wait_ge(sm("con_in"), 16)
            pool.wait_ge(sm("sq_used"), 4)
            step.link(pool.tensor_copy(ang, rope1[:, 1].bitcast(mybir.dt.int32)))
            step.link(pool.tensor_scalar(ang, ang, con[:, C_INVF:C_INVF + 1], None, ALU.mult))
            for turn in range(2):
                step.link(pool.tensor_scalar(n, ang, float(1 / TWO_PI), ROUND, ALU.mult, ALU.add))
                step.link(pool.tensor_scalar(n, n, -ROUND, None, ALU.add))
                for part in parts:
                    step.link(pool.tensor_scalar(prod, n, part, None, ALU.mult))
                    step.link(pool.tensor_tensor(ang, ang, prod, ALU.subtract))
            step.link(pool.tensor_scalar(n, ang, float(np.pi / 2), -TWO_PI, ALU.is_gt, ALU.mult))
            step.link(pool.tensor_tensor(n, n, ang, ALU.add))
            step.link(pool.tensor_scalar(n, n, float(np.pi / 2), 3.1415925, ALU.add, ALU.min))
            step.link(pool.tensor_scalar(n, n, -3.1415925, None, ALU.max))
            step.link(pool.tensor_scalar(ang, ang, 3.1415925, -3.1415925, ALU.min, ALU.max))
            pool.sem_inc(sm("angles"), 1)

            def normed_add(dst, gain, ready):
                step.link(pool.tensor_tensor(pool_tmp, acc[:, 6:8], bc2(rstd[:, :]), ALU.mult))
                for n in range(2):
                    ins = pool.tensor_scalar(pool_tmp[:, n], pool_tmp[:, n], col2[:, gain + 6 + n:gain + 7 + n], None,
                                             ALU.mult)
                step.link(ins)
                pool.tensor_tensor(dst, pool_tmp, X[:, 6:8], ALU.add).then_inc(sm(ready), 1)
                pool.wait_ge(sm(ready), 1)

            for k in POOL_SQ:
                if k == 16:
                    pool.wait_ge(sm("rstd_ready"), 3)
                    pool.wait_ge(sm("x_split"), X_H3 + 4)
                    for j in range(4):
                        xp = X[:, 2 * j:2 * j + 2]
                        step.link(pool.tensor_tensor(xp, xp, bc2(rope1[:, 0]), ALU.mult))
                        for c in (2 * j, 2 * j + 1):
                            ins = pool.tensor_scalar(X[:, c], X[:, c], col1[:, 64 + c:65 + c], None, ALU.mult)
                        ins.then_inc(sm("x_block1"), 1)
                        pool.wait_ge(sm("x_block1"), j + 1)
                if k == 20:
                    pool.wait_ge(sm("rstd_ready"), 4)
                    normed_add(X[:, 6:8], 8, "x_new_last")
                pool.wait_ge(sm("sq_ready"), k + 1)
                s, (o, first) = sq_buf(k), POOL_SQ[k]
                if first:
                    pool.tensor_tensor(sq_sum[o], s[:, 0], s[:, 1], ALU.add).then_inc(sm("sq_used"), 1)
                else:
                    step.link(pool.tensor_tensor(sq_sum[o], sq_sum[o], s[:, 0], ALU.add))
                    pool.tensor_tensor(sq_sum[o], sq_sum[o], s[:, 1], ALU.add).then_inc(sm("sq_used"), 1)
                pool.wait_ge(sm("sq_used"), k + 1)
            pool.wait_ge(sm("rstd_ready"), 6)
            normed_add(acc[:, 6:8], 24, "result_last")

        @block.scalar
        def _(act):
            step = Steps(act, sm("act_step"))
            a = act.activation

            def hi(u, p):
                act.wait_ge(sm(f"raw_in{p}"), 8 * u - 8 * p + 16)
                act.wait_ge(sm("unit_done"), free(u))
                a(w_hi[:, p], raw[:, p], ACT.Copy).then_inc(sm("hi_split"), 1)

            def split_hi(dst, src, scale=1.0):
                return a(dst, src, ACT.Copy, scale=scale).then_inc(sm("x_hi"), 1)

            def rms(n_sq, bank, dst=rstd, width=D, ready="rstd_ready"):
                act.wait_ge(sm("sq_used"), n_sq)
                step.link(a(dst[:, :], T[:, bank], ACT.Ln, scale=1.0 / width, bias=EPS))
                a(dst[:, :], dst[:, :], ACT.Exp, scale=-0.5).then_inc(sm(ready), 1)

            def squares(k, src):
                if k >= 2:
                    act.wait_ge(sm("sq_used"), k - 1)
                a(sq_buf(k), src, ACT.Square).then_inc(sm("sq_ready"), 1)

            act.wait_ge(sm("col1_ready"), 1)
            a(cs[:, :], col1[:, 96:104], ACT.Silu).then_inc(sm("cs_ready"), 1)
            for t in range(KC):
                act.wait_ge(sm("x_t"), t + 1)
                a(X[:, t], G[:, t % 4], ACT.Copy).then_inc(sm("x_ready"), 1)
            for j in range(4):
                act.wait_ge(sm("x_ready"), 2 * j + 2)
                squares(j, X[:, 2 * j:2 * j + 2])
            rms(4, 1)
            hi(0, 0)
            act.wait_ge(sm("xr_ready"), 4)
            for j in range(4):
                act.wait_ge(sm("gs_ready"), j + 1)
                for c in (2 * j, 2 * j + 1):
                    ins = a(h_hi[:, c], xr[:, c], ACT.Identity, scale=gs[:, c:c + 1], bias=mod[:, c:c + 1])
                ins.then_inc(sm("x_hi"), 1)
            with act.Fori(0, 2) as i:
                for jj in range(2):
                    for m in range(3):
                        k = 3 * jj + m
                        u = U_CONV + 6 * i + k
                        j = 2 * i + jj
                        hi(u + 1, (k + 1) % 2)
                        if m == 1:
                            act.wait_ge(sm("evac"), done(u))
                            for n in range(2):
                                ins = a(cv[:, n], u_pad[:, n, 0:S], ACT.Copy,
                                        scale=col1[:, bass.ds(72 + 2 * j + n, 1)])
                            ins.then_inc(sm("conv0"), 1)
                        if m == 2:
                            act.wait_ge(sm("evac"), done(u))
                            split_hi(ga_hi[:, bass.ds(2 * j, 2), :], cv)
            act.wait_ge(sm("angles"), 1)
            step.link(a(small_rope, rope1[:, 0], ACT.Sin))
            step.link(a(rope1[:, 0], rope1[:, 1], ACT.Sin))
            step.link(a(rope1[0:64, 1], small_rope[0:64, :], ACT.Copy, scale=-1.0))
            a(rope1[64:128, 1], small_rope[64:128, :], ACT.Copy).then_inc(sm("rope_ready"), 1)
            with act.Fori(0, 4) as i:
                u = U_COUT + 2 * i
                hi(u + 1, 1)
                act.wait_ge(sm("unit_done"), done(u))
                act.wait_ge(sm("evac"), free(u) + 1)
                a(tmp[:, :, :], ps(0), ACT.Sigmoid).then_inc(sm("gb_ready"), 1)
                hi(u + 2, 0)
            hi(U_RET + 1, 1)
            with step.loop(0, 4, 1) as i:
                u = U_RET + 4 * i
                for m in range(2):
                    if m == 1:
                        hi(u + 2, 0)
                    act.wait_ge(sm("unit_done"), done(u + m))
                    if m == 0:
                        act.wait_ge(sm("evac"), free(u) + 1)
                    else:
                        act.wait_ge(sm("rotated"), 2 * i + 1)
                    a(sw[64:128], G[0:64, 2 * m:2 * m + 2], ACT.Copy)
                    a(sw[0:64], G[64:128, 2 * m:2 * m + 2], ACT.Copy).then_inc(sm("swapped"), 1)
                hi(u + 3, 1)
                hi(u + 4, 0)
                act.wait_ge(sm("pv_done"), 2 * i + 2)
                a(sqp[:, :, :], T[:, 2:4], ACT.Square).then_inc(sm("ysq_ready"), 1)
                act.wait_ge(sm("unit_done"), done(u + 3))
                a(gg, ps(1), ACT.Silu).then_inc(sm("g_ready"), 1)
                hi(u + 5, 1)
                act.wait_ge(sm("var_done"), i + 1)
                step.link(a(sw, T[:, 0:2], ACT.Ln, scale=1.0 / HEAD, bias=EPS))
                a(sw, sw, ACT.Exp, scale=-0.5).then_inc(sm("y_rstd"), 1)
                act.wait_ge(sm("ret_ready"), i + 1)
                split_hi(ga_hi[:, bass.ds(2 * i, 2), :], tmp[:, :, :])
            with act.Fori(0, 2) as i:
                for m in range(2):
                    u = U_GA + 2 * i + m
                    act.wait_ge(sm("unit_done"), done(u))
                    a(sga[:, bass.ds(4 * i + 2 * m, 2), :], ps(m), ACT.Sigmoid).then_inc(sm("ga_ready"), 1)
                    hi(u + 2, m)
            with act.Fori(0, 2) as i:
                for m in range(2):
                    u = U_ROUT + 2 * i + m
                    act.wait_ge(sm("merged"), 2 * i + m + 1)
                    split_hi(h_hi[:, bass.ds(4 * i + 2 * m, 2), :], tmp[:, :, :])
                    hi(u + 2, m)
            for j in range(4):
                u = U_MIX + j
                if j >= 1:
                    hi(u + 1, (u + 1) % 2)
                act.wait_ge(sm("evac"), done(u))
                squares(4 + j, X[:, 2 * j:2 * j + 2])
            rms(8, 0)
            for j in range(4):
                act.wait_ge(sm("x32"), 4 + j + 1)
                for n in range(2):
                    c = 2 * j + n
                    ins = a(h_hi[:, c], norm_tmp[j % 2][:, n], ACT.Identity, bias=mod[:, 24 + c:25 + c])
                ins.then_inc(sm("x_hi"), 1)

            def ffn_up(u, pairs, xb):
                with act.Fori(0, pairs) as i:
                    hi(u + 2 * i + 1, 1)
                    act.wait_ge(sm("unit_done"), done(u + 2 * i))
                    act.wait_ge(sm("evac"), free(u + 2 * i) + 1)
                    a(gate, ps(0), ACT.Silu).then_inc(sm("gate_ready"), 1)
                    hi(u + 2 * i + 2, 0)
                    act.wait_ge(sm("evac"), done(u + 2 * i + 1))
                    split_hi(ga_hi[:, bass.ds(2 * i, 2), :], tmp[:, :, :])

            with act.Fori(0, 2) as g:
                ffn_up(U_FFN + 12 * g, 4, None)
                with act.Fori(0, 2) as i:
                    for m in range(2):
                        hi(U_FFN + 12 * g + 8 + 2 * i + m + 1, 1 - m)
            ffn_up(U_FFN + 24, 3, None)
            for j in range(4):
                u = U_FFN + 30 + j
                if j == 0:
                    hi(u + 1, (u + 1) % 2)
                act.wait_ge(sm("evac"), done(u))
                for n in range(2):
                    c = 2 * j + n
                    ins = a(h_hi[:, c], X[:, c], ACT.Copy, scale=gain12[:, c:c + 1])
                ins.then_inc(sm("x_hi"), 1)
                if j < 3:
                    hi(u + 2, u % 2)
                squares(8 + 2 * j, X[:, 2 * j:2 * j + 2])
                act.wait_ge(sm("sq_used"), 8 + 2 * j)
                for n in range(2):
                    ins = a(spare[:, n], X[:, 2 * j + n], ACT.Square, scale=col1[:, 64 + 2 * j + n:65 + 2 * j + n])
                ins.then_inc(sm("sq_ready"), 1)
            hi(U_IN2 + 1, 1)
            act.wait_ge(sm("gate_w_in"), 16)
            hi(U_IN2 + 2, 0)
            rms(16, 0, rope1[:, 0])
            act.wait_ge(sm("sq2_ready"), 1)
            step.link(a(rstd[:, :], rstd[:, :], ACT.Ln, scale=1.0 / D, bias=EPS))
            a(rstd[:, :], rstd[:, :], ACT.Exp, scale=-0.5).then_inc(sm("rstd2_ready"), 1)
            act.wait_ge(sm("lam_dots"), 1)
            a(lam_row[:, 2:4], lam_row[:, 0:2], ACT.Exp).then_inc(sm("lam_exp"), 1)

            def evac2(k):
                u, kind = U_IN2 + k, IN2[k]
                p = u % 2
                if kind[:2] in ("dq", "dk"):
                    n = ("dq0", "dk0", "dq1", "dk1").index(kind)
                    act.wait_ge(sm("unit_done"), done(u))
                    if n >= 1:
                        act.wait_ge(sm("rotated2"), n)
                    for b in (0, 64):
                        a(sqp[b + 32:b + 64], G[b:b + 32, 2 * p:2 * p + 2], ACT.Copy)
                        ins = a(sqp[b:b + 32], G[b + 32:b + 64, 2 * p:2 * p + 2], ACT.Copy)
                    ins.then_inc(sm("swapped2"), 1)
                elif kind in ("mo0", "mo1"):
                    n = int(kind[2])
                    act.wait_ge(sm("evac"), done(u))
                    a(mo[:, 2 * n:2 * n + 2], mo[:, 2 * n:2 * n + 2], ACT.Sigmoid).then_inc(sm("mo_ready"), 1)

            for k in range(5):
                u = U_IN2 + k
                if k == 1:
                    hi(u + 2, (u + 2) % 2)
                if k >= 3:
                    hi(u + 1, (u + 1) % 2)
                if k == 3:
                    act.wait_ge(sm("f_pre"), 1)
                    step.link(a(lf_row, f_row, ACT.Abs))
                    step.link(a(lf_row, lf_row, ACT.Exp, scale=-1.0))
                    a(lf_row, lf_row, ACT.Ln, bias=1.0).then_inc(sm("softplus"), 1)
                if k in (0, 1):
                    act.wait_ge(sm("evac"), done(u))
                    i = k
                    for n in range(2):
                        ins = a(mqk[i][:, n], m_pad[:, n, 0:S], ACT.Identity,
                                scale=col2[:, 32 + 2 * i + n:33 + 2 * i + n], bias=col2[:, 48 + 2 * i + n:49 + 2 * i + n])
                    ins.then_inc(sm("mconv0"), 1)
                if k in (1, 2):
                    act.wait_ge(sm("mconv"), k)
                    a(mqk[k - 1], mqk[k - 1], ACT.Silu).then_inc(sm("mqk_ready"), 1)

            act.wait_ge(sm("a_cols"), 1)
            act.wait_ge(sm("x_block1"), 4)
            for h in range(4):
                k = 5 + 2 * h
                act.wait_ge(sm("m_bcast"), h + 1)
                if h >= 1:
                    act.wait_ge(sm("m_out"), h)
                a(nm, T[:, 3], ACT.Copy).then_inc(sm("nm_ready"), 1)
                hi(U_IN2 + k + 1, (k + 1) % 2)
                evac2(k - 1)
                act.wait_ge(sm("nmd_ready"), h + 1)
                for b in range(NB):
                    bias = a_col[:, 4 * b + h:4 * b + h + 1]
                    ins = a(pm[b][:, 0:P], nmd[:, P * b:P * b + P], ACT.Exp, bias=bias)
                    if b < NB - 1:
                        ins = a(pm[b][:, P:TRI[b]], nm[:, P * (b + 1):S], ACT.Exp, bias=bias)
                ins.then_inc(sm("dm_ready"), 1)
                evac2(k)
                hi(U_IN2 + k + 2, k % 2)
                act.wait_ge(sm("num_done"), h + 1)
                a(em2[:, :], T[:, 3], ACT.Exp, scale=-2.0)
                a(nmd, T[:, 1], ACT.Square)
                a(nm, T[:, 0], ACT.Square).then_inc(sm("msq_ready"), 1)
                act.wait_ge(sm("mvar_ready"), h + 1)
                step.link(a(em2[:, :], em2[:, :], ACT.Ln, scale=1.0 / HEAD))
                a(em2[:, :], em2[:, :], ACT.Exp, scale=-0.5).then_inc(sm("m_rstd"), 1)
                act.wait_ge(sm("m_out"), h + 1)
                split_hi(ga_hi[:, 4 + h], tmp[:, 0])

            def softmax_exp(h, c):
                bank = T if c == 0 else G
                act.wait_ge(sm("nmax"), 2 * h + c + 1)
                for b in range(NB):
                    wd = P * (b + 1)
                    q, at = Q_BANK[b]
                    k = slice(4 * c + b, 4 * c + b + 1)
                    ins = a(pr[h % 2][c][:, QAT[b]:QAT[b] + wd], bank[:, q, at:at + wd], ACT.Exp, scale=DQK ** -0.5,
                            bias=nmax[h % 2][:, k], accum_out=sums[h % 2][:, k])
                ins.then_inc(sm("p_ready"), 1)

            def turned_copy(h, blocks):
                for b in blocks:
                    ins = a(pt[:, TRI_AT[b]:TRI_AT[b] + TRI[b]], turned(h, b), ACT.Copy)
                ins.then_inc(sm("pt_ready"), 1)

            softmax_exp(0, 0)
            softmax_exp(0, 1)
            hi(U_OUT2 + 1, (U_OUT2 + 1) % 2)
            for h in range(4):
                act.wait_ge(sm("p_turned"), 2 * h + 1)
                turned_copy(h, (0, 1, 3))
                if h == 0:
                    softmax_exp(1, 0)
                act.wait_ge(sm("p_turned"), 2 * h + 2)
                turned_copy(h, (2,))
                if 1 <= h < 3:
                    softmax_exp(h + 1, 0)
                if h in (0, 2):
                    softmax_exp(h + 1, 1)
                act.wait_ge(sm("dpv_done"), h + 1)
                a(dsq, pv_bank(h), ACT.Square).then_inc(sm("dsq_ready"), 1)
                if h == 1:
                    softmax_exp(2, 1)
                act.wait_ge(sm("dvar_done"), h + 1)
                step.link(a(drs, var_bank(h), ACT.Ln, scale=1.0 / HEAD, bias=EPS))
                a(drs, drs, ACT.Exp, scale=-0.5).then_inc(sm("d_rstd"), 1)
                act.wait_ge(sm("d_out"), h + 1)
                split_hi(ga_hi[:, h], tmp[:, h % 2], scale=dgain[:, 0:1])

            for j in range(4):
                u = U_OUT2 + j
                if j < 3:
                    hi(u + 2, u % 2)
                act.wait_ge(sm("evac"), done(u))
                squares(16 + j, acc[:, 2 * j:2 * j + 2])
            rms(20, 0)
            for j in range(4):
                if j < 3:
                    act.wait_ge(sm("x_new"), j + 1)
                else:
                    act.wait_ge(sm("x_new_last"), 1)
                for n in range(2):
                    c = 2 * j + n
                    ins = a(h2_hi[:, c], X[:, c], ACT.Copy, scale=col2[:, 16 + c:17 + c])
                ins.then_inc(sm("x_hi"), 1)
                squares(20 + j, X[:, 2 * j:2 * j + 2])

            def mlp_up(u, first=False):
                for m in range(4):
                    p = (U_MLP + m) % 2
                    hi(u + m + 1, 1 - p)
                    if first and m == 0:
                        rms(24, 1)
                    act.wait_ge(sm("evac"), done(u + m))
                    a(ga_hi[:, 2 * m:2 * m + 2], tmp[:, :, :], ACT.Square).then_inc(sm("x_hi"), 1)

            def mlp(u, first=False):
                mlp_up(u, first)
                for m in range(4):
                    hi(u + 5 + m, (U_MLP + m + 1) % 2)

            mlp(U_MLP, True)
            with act.Fori(1, 3) as g:
                mlp(U_MLP + 8 * g)
            mlp_up(U_MLP + 24)
            for j in range(4):
                u = U_MLP + 28 + j
                if u + 1 < U_END:
                    hi(u + 1, (u + 1) % 2)
                act.wait_ge(sm("evac"), done(u))
                squares(24 + j, acc[:, 2 * j:2 * j + 2])
            rms(28, 0)
            for j in range(4):
                act.wait_ge(sm("out_turned"), j + 1)
                a(out_tok[:, :, j * UC:(j + 1) * UC],
                  G[:, 2 * (j % 2):2 * (j % 2) + 2].rearrange("p a (b c) -> p (a b) c", b=2), ACT.Copy)\
                    .then_inc(sm("out_ready"), 1)

        @block.vector
        def _(dve):
            step = Steps(dve, sm("dve_step"))
            tt, ts, stt, cp = dve.tensor_tensor, dve.tensor_scalar, dve.scalar_tensor_tensor, dve.tensor_copy

            for name in ("lo_split", "unit_done", "evac", "ada_used", "scores_used"):
                dve.sem_inc(sm(name), BUFS)

            def lo(u, p):
                dve.wait_ge(sm("hi_split"), u + 1)
                tt(w_lo[:, p], raw[:, p], w_hi[:, p].bitcast(F32), ALU.subtract).then_inc(sm("lo_split"), 1)

            def evacuated(u):
                dve.wait_ge(sm("evac"), done(u - 1))
                dve.sem_inc(sm("evac"), 1)

            def split_lo(k, dst, src, hi_part):
                dve.wait_ge(sm("x_hi"), k + 1)
                tt(dst, src, hi_part.bitcast(F32), ALU.subtract).then_inc(sm("x_split"), 1)
                dve.wait_ge(sm("x_split"), k + 1)

            def ada_add(a, p, t):
                dve.wait_ge(sm(f"ada_in{p}"), 8 * (a - KC) - 8 * p + 16)
                stt(ada_sum, ada[:, p], cs[:, bass.ds(t, 1)], ada_sum, ALU.mult, ALU.add).then_inc(sm("ada_used"), 1)
                dve.wait_ge(sm("ada_used"), done(a))

            def ada_cols(third):
                dve.wait_ge(sm("mod_done"), third)
                step.link(tt(mod[:, 16 * third:16 * third + 16], T[:, 0, 0:16],
                             col1[:, 16 * third:16 * third + 16], ALU.add))

            dve.wait_ge(sm("turned1"), 1)
            cp(col1[:, :], T[:, 0, 0:N1]).then_inc(sm("col1_ready"), 1)
            step.link(dve.memset(ada_sum, 0.0))
            dve.wait_ge(sm("cs_ready"), 1)
            for t in range(KC):
                dve.wait_ge(sm(f"ada_first{t % FIRST_SLOTS}"), 16 * (t // FIRST_SLOTS) + 16)
                stt(ada_sum, ada_first(t), cs[:, t:t + 1], ada_sum, ALU.mult, ALU.add).then_inc(sm("ada_used"), 1)
                dve.wait_ge(sm("ada_used"), done(t))
            dve.wait_ge(sm("turned2"), 1)
            cp(col2[:, :], T[:, 2, 0:N2]).then_inc(sm("col2_ready"), 1)
            dve.wait_ge(sm("col2_ready"), 1)
            tt(gain12, col1[:, 64:72], col2[:, 0:8], ALU.mult).then_inc(sm("gain12_ready"), 1)
            dve.wait_ge(sm("gain12_ready"), 1)
            dve.wait_ge(sm("xr_ready"), 4)
            for j in range(5):
                if j < 4:
                    dve.wait_ge(sm("mod1_part"), j + 1)
                    for k in (2 * j, 8 + 2 * j):
                        ins = tt(mod[:, k:k + 2], T[:, j, k:k + 2], col1[:, k:k + 2], ALU.add)
                    step.link(ins)
                    k = slice(2 * j, 2 * j + 2)
                    stt(gs[:, k], mod[:, 8 + 2 * j:10 + 2 * j], 1.0, col1[:, 48 + 2 * j:50 + 2 * j], ALU.add, ALU.mult)\
                        .then_inc(sm("gs_ready"), 1)
                    dve.wait_ge(sm("gs_ready"), j + 1)
                    for n in range(2):
                        c = 2 * j + n
                        ins = ts(norm_tmp[j % 2][:, n], xr[:, c], gs[:, c:c + 1], mod[:, c:c + 1], ALU.mult, ALU.add)
                    ins.then_inc(sm("x32"), 1)
                if j == 0:
                    lo(0, 0)
                else:
                    c = slice(2 * j - 2, 2 * j)
                    dve.wait_ge(sm("x32"), j)
                    split_lo(X_H1 + j - 1, h_lo[:, c], norm_tmp[(j - 1) % 2], h_hi[:, c])
            step.link(dve.memset(ada_sum, 0.0))

            with step.loop(0, 2, 4) as i:
                for jj in range(2):
                    for m in range(3):
                        k = 3 * jj + m
                        u = U_CONV + 6 * i + k
                        j = 2 * i + jj
                        p = k % 2
                        lo(u + 1, 1 - p)
                        dve.wait_ge(sm("unit_done"), done(u))
                        if m == 0:
                            cp(u_cv, ps(p)).then_inc(sm("evac"), 1)
                        elif m == 1:
                            if k == 1:
                                dve.wait_ge(sm("pads"), 1)
                            dve.wait_ge(sm("evac"), done(u - 1))
                            tt(u_pad[:, :, 2:2 + S], ps(p), u_cv, ALU.mult).then_inc(sm("evac"), 1)
                            dve.wait_ge(sm("evac"), done(u))
                            dve.wait_ge(sm("conv0"), j + 1)
                            for tap in (1, 2):
                                for n in range(2):
                                    ins = stt(cv[:, n], u_pad[:, n, tap:tap + S],
                                              col1[:, bass.ds(72 + 8 * tap + 2 * j + n, 1)], cv[:, n],
                                              ALU.mult, ALU.add)
                                step.link(ins)
                        else:
                            tt(cv, ps(p), cv, ALU.mult).then_inc(sm("evac"), 1)
                            dve.wait_ge(sm("evac"), done(u))
                            split_lo(X_CV + j, ga_lo[:, bass.ds(2 * j, 2), :], cv, ga_hi[:, bass.ds(2 * j, 2), :])
                        if k < 4:
                            ada_add(8 + 4 * i + k, k % 2, 4 * i + k)
            dve.wait_ge(sm("mod_done"), 1)
            step.link(dve.memset(ada_sum, 0.0))
            ada_cols(1)
            with dve.Fori(0, 4) as i:
                u = U_COUT + 2 * i
                lo(u + 1, 1)
                ada_add(16 + 2 * i, 0, 2 * i)
                dve.wait_ge(sm("gb_ready"), i + 1)
                evacuated(u)
                lo(u + 2, 0)
                ada_add(17 + 2 * i, 1, 2 * i + 1)
                dve.wait_ge(sm("unit_done"), done(u + 1))
                tt(acc[:, bass.ds(2 * i, 2), :], ps(1), tmp[:, :, :], ALU.mult).then_inc(sm("evac"), 1)
            ada_cols(2)
            step.link(stt(gs[:, 8:16], mod[:, 32:40], 1.0, col1[:, 56:64], ALU.add, ALU.mult))
            dve.wait_ge(sm("rope_ready"), 1)
            lo(U_RET + 1, 1)
            with step.loop(0, 4, 5) as i:
                u = U_RET + 4 * i
                for m, dst in ((0, qq), (1, kk)):
                    if m == 1:
                        lo(u + 2, 0)
                    dve.wait_ge(sm("swapped"), 2 * i + m + 1)
                    tt(dst, ps(m), bc2(rope1[:, 0]), ALU.mult).then_inc(sm("evac"), 1)
                    step.link(tt(sw, sw, bc2(rope1[:, 1]), ALU.mult))
                    dve.wait_ge(sm("evac"), done(u + m))
                    tt(dst, dst, sw, ALU.add).then_inc(sm("rotated"), 1)
                lo(u + 3, 1)

                def decayed(h):
                    dve.wait_ge(sm("scores"), 2 * i + h + 1)
                    for b in range(NB):
                        bank, at = S_BANK[b]
                        ins = tt(pp[h][:, TRI_AT[b]:TRI_AT[b] + TRI[b]], T[:, bank, at:at + TRI[b]],
                                 decay[:, h, 0:TRI[b]], ALU.mult)
                    ins.then_inc(sm("scores_used"), 1)

                dve.wait_ge(sm("decay_in"), 16 * i + 16)
                decayed(0)
                dve.wait_ge(sm("unit_done"), done(u + 2))
                v_ps = ps(0).rearrange("p a (b h c) -> p (a b h) c", b=2, h=2)
                step.link(dve.tensor_reduce(v_mean, v_ps, AX.X, ALU.add))
                step.link(ts(v_mean, v_mean, 1.0 / HEAD, None, ALU.mult))
                tt(vv.rearrange("p b (h c) -> p (b h) c", h=2), v_ps,
                   v_mean.unsqueeze(2).to_broadcast([P, 2 * NB, HEAD]), ALU.subtract).then_inc(sm("evac"), 1)
                decayed(1)
                lo(u + 4, 0)
                dve.wait_ge(sm("g_ready"), i + 1)
                evacuated(u + 3)
                lo(u + 5, 1)
                dve.wait_ge(sm("y_rstd"), i + 1)
                step.link(tt(tmp[:, :, :], T[:, 2:4], sw, ALU.mult))
                tt(tmp[:, :, :], tmp[:, :, :], gg, ALU.mult).then_inc(sm("ret_ready"), 1)
                dve.wait_ge(sm("ret_ready"), i + 1)
                split_lo(X_RET + i, ga_lo[:, bass.ds(2 * i, 2), :], tmp[:, :, :], ga_hi[:, bass.ds(2 * i, 2), :])
            with dve.Fori(0, 2) as i:
                for m in range(2):
                    dve.wait_ge(sm("ga_ready"), 2 * i + m + 1)
                    evacuated(U_GA + 2 * i + m)
                    lo(U_GA + 2 * i + m + 2, m)
            with dve.Fori(0, 2) as i:
                for m in range(2):
                    u = U_ROUT + 2 * i + m
                    c = bass.ds(4 * i + 2 * m, 2)
                    dve.wait_ge(sm("unit_done"), done(u))
                    tt(tmp[:, :, :], ps(m), sga[:, c, :], ALU.mult).then_inc(sm("evac"), 1)
                    dve.wait_ge(sm("evac"), done(u))
                    tt(tmp[:, :, :], tmp[:, :, :], acc[:, c, :], ALU.add).then_inc(sm("merged"), 1)
                    dve.wait_ge(sm("merged"), 2 * i + m + 1)
                    split_lo(X_MRG + 2 * i + m, h_lo[:, c, :], tmp[:, :, :], h_hi[:, c, :])
                    lo(u + 2, m)

            def add_pair(u, j, p, gain):
                dve.wait_ge(sm("unit_done"), done(u))
                for n in range(2):
                    c = bass.ds(2 * j + n, 1) if not isinstance(j, int) else slice(2 * j + n, 2 * j + n + 1)
                    gcol = mod[:, bass.ds(gain + 2 * j + n, 1)]
                    ins = stt(X[:, c, :][:, 0], G[:, 2 * p + n], gcol, X[:, c, :][:, 0], ALU.mult, ALU.add)
                ins.then_inc(sm("evac"), 1)

            for j in range(4):
                u = U_MIX + j
                if j >= 1:
                    lo(u + 1, (u + 1) % 2)
                add_pair(u, j, u % 2, 16)
                dve.wait_ge(sm("evac"), done(u))
                for c in (2 * j, 2 * j + 1):
                    ins = ts(xg[:, c], X[:, c], gs[:, 8 + c:9 + c], None, ALU.mult)
                step.link(ins)
            dve.wait_ge(sm("rstd_ready"), 2)
            for j in range(5):
                if j < 4:
                    tt(norm_tmp[j % 2], xg[:, 2 * j:2 * j + 2], bc2(rstd[:, :]), ALU.mult).then_inc(sm("x32"), 1)
                if j >= 1:
                    dve.wait_ge(sm("x32"), 4 + j)
                    dve.wait_ge(sm("x_hi"), X_H2 + j)
                    for n in range(2):
                        c = 2 * j - 2 + n
                        ins = stt(h_lo[:, c], norm_tmp[(j - 1) % 2][:, n], mod[:, 24 + c:25 + c],
                                  h_hi[:, c].bitcast(F32), ALU.add, ALU.subtract)
                    ins.then_inc(sm("x_split"), 1)
                    dve.wait_ge(sm("x_split"), X_H2 + j)

            def ffn_up(u, pairs, xk, gk):
                with dve.Fori(0, pairs) as i:
                    lo(u + 2 * i + 1, 1)
                    dve.wait_ge(sm("gate_ready"), gk + i + 1)
                    evacuated(u + 2 * i)
                    lo(u + 2 * i + 2, 0)
                    dve.wait_ge(sm("unit_done"), done(u + 2 * i + 1))
                    tt(tmp[:, :, :], ps(1), gate, ALU.mult).then_inc(sm("evac"), 1)
                    dve.wait_ge(sm("evac"), done(u + 2 * i + 1))
                    split_lo(xk + i, ga_lo[:, bass.ds(2 * i, 2), :], tmp[:, :, :], ga_hi[:, bass.ds(2 * i, 2), :])

            with dve.Fori(0, 2) as g:
                u = U_FFN + 12 * g
                ffn_up(u, 4, X_HID + 4 * g, 4 * g)
                with dve.Fori(0, 2) as i:
                    for m in range(2):
                        v = u + 8 + 2 * i + m
                        lo(v + 1, 1 - m)
                        add_pair(v, 2 * i + m, m, 40)
            ffn_up(U_FFN + 24, 3, X_HID + 8, 8)

            def scaled_lo(k, dst, hi_part, gain, j):
                dve.wait_ge(sm("x_hi"), k + 1)
                for n in range(2):
                    c = 2 * j + n
                    ins = stt(dst[:, c], X[:, c], gain[:, c:c + 1], hi_part[:, c].bitcast(F32), ALU.mult, ALU.subtract)
                ins.then_inc(sm("x_split"), 1)
                dve.wait_ge(sm("x_split"), k + 1)

            for j in range(4):
                u = U_FFN + 30 + j
                lo(u + 1, (u + 1) % 2)
                add_pair(u, j, u % 2, 40)
                dve.wait_ge(sm("evac"), done(u))
                scaled_lo(X_H3 + j, h_lo, h_hi, gain12, j)
            dve.wait_ge(sm("par2_in"), 16 * (len(PAR2) + 6))
            lr = par2[0:1, P:4 * P]
            step.link(tt(lr[:, 256:320], lr[:, 0:64], lr[:, 64:128], ALU.mult))
            step.link(tt(lr[:, 320:384], lr[:, 128:192], lr[:, 192:256], ALU.mult))
            dve.tensor_reduce(lam_row[:, 0:2], lr[:, 256:384].rearrange("p (a b) -> p a b", a=2), AX.X, ALU.add)\
                .then_inc(sm("lam_dots"), 1)
            lo(U_IN2 + 1, 1)
            lo(U_IN2 + 2, 0)
            r1 = rope1[:, 0]
            dve.wait_ge(sm("rstd_ready"), 3)
            step.link(tt(rstd[:, :], r1, r1, ALU.mult))
            tt(rstd[:, :], rstd[:, :], T[:, 1], ALU.mult).then_inc(sm("sq2_ready"), 1)
            dve.wait_ge(sm("rstd2_ready"), 1)
            tt(rstd[:, :], rstd[:, :], r1, ALU.mult).then_inc(sm("r12_ready"), 1)
            dve.wait_ge(sm("r12_ready"), 1)

            def evac2(k):
                u, kind = U_IN2 + k, IN2[k]
                p = u % 2
                if kind[:2] in ("dq", "dk"):
                    n = ("dq0", "dk0", "dq1", "dk1").index(kind)
                    dst = (q2, k2)[n % 2][:, 2 * (n // 2):2 * (n // 2) + 2]
                    dve.wait_ge(sm("swapped2"), n + 1)
                    tt(dst, ps(p), bc2(cos2), ALU.mult).then_inc(sm("evac"), 1)
                    step.link(tt(sqp[:, :, :], sqp[:, :, :], bc2(sin2), ALU.mult))
                    dve.wait_ge(sm("evac"), done(u))
                    tt(dst, dst, sqp[:, :, :], ALU.add).then_inc(sm("rotated2"), 1)
                elif kind[1] == "v":
                    dst, n = (vd if kind[0] == "d" else vm), int(kind[2])
                    dve.wait_ge(sm("unit_done"), done(u))
                    if kind == "mv0":
                        dve.wait_ge(sm("r12_turned"), 1)
                        step.link(cp(r12_col, T[:, 2, 0:NB]))
                    for b in range(NB):
                        ins = ts(dst[:, b, n * UC:(n + 1) * UC], G[:, 2 * p + b // 2, (b % 2) * UC:(b % 2 + 1) * UC],
                                 r12_col[:, b:b + 1], None, ALU.mult)
                    ins.then_inc(sm("evac"), 1)
                elif kind in ("mq", "mk"):
                    i = k
                    dve.wait_ge(sm("unit_done"), done(u))
                    dve.wait_ge(sm("mpads"), 1)
                    if i == 1:
                        dve.wait_ge(sm("mconv"), 1)
                    tt(m_pad[:, :, 3:3 + S], ps(p), bc2(rstd[:, :]), ALU.mult).then_inc(sm("evac"), 1)
                    dve.wait_ge(sm("evac"), done(u))
                    dve.wait_ge(sm("mconv0"), i + 1)
                    for tap in (1, 2, 3):
                        for n in range(2):
                            ins = stt(mqk[i][:, n], m_pad[:, n, tap:tap + S],
                                      col2[:, 32 + 4 * tap + 2 * i + n:33 + 4 * tap + 2 * i + n], mqk[i][:, n],
                                      ALU.mult, ALU.add)
                        if tap < 3:
                            step.link(ins)
                    ins.then_inc(sm("mconv"), 1)
                elif kind == "gates":
                    dve.wait_ge(sm("unit_done"), done(u))
                    tt(i_row, G[0:4, 2 * p], rstd[0:4, :], ALU.mult)
                    tt(f_row, G[32:36, 2 * p], rstd[32:36, :], ALU.mult).then_inc(sm("evac"), 1)
                else:
                    n = int(kind[2])
                    dve.wait_ge(sm("unit_done"), done(u))
                    tt(mo[:, 2 * n:2 * n + 2], ps(p), bc2(rstd[:, :]), ALU.mult).then_inc(sm("evac"), 1)

            for k in range(5):
                u = U_IN2 + k
                if k == 1:
                    lo(u + 2, (u + 2) % 2)
                if k == 4:
                    lo(u + 1, (u + 1) % 2)
                if k == 0:
                    dve.memset(m_pad[:, :, 0:3], 0.0).then_inc(sm("mpads"), 1)
                elif k == 1:
                    dve.wait_ge(sm("lam_exp"), 1)
                    step.link(tt(lam_row[:, 4:5], lam_row[:, 3:4], lam_row[:, 2:3], ALU.subtract))
                    ts(lam_row[:, 5:6], lam_row[:, 4:5], -LAMBDA_INIT, None, ALU.add).then_inc(sm("lam_ready"), 1)
                    step.link(ts(dgain[:, 0:1], col2[:, 52:53], 1.0 - LAMBDA_INIT, None, ALU.mult))
                elif k == 4:
                    step.link(tt(cos2, cos2, rstd[:, :], ALU.mult))
                    step.link(tt(sin2, sin2, rstd[:, :], ALU.mult))
                elif k == 3:
                    dve.wait_ge(sm("evac"), done(U_IN2 + 2))
                    step.link(ts(f_row, f_row, small[0:4, 33:34], None, ALU.add))
                    dve.sem_inc(sm("f_pre"), 1)
                    step.link(ts(i_row, i_row, small[0:4, 32:33], None, ALU.add))
                    step.link(ts(f_row2, f_row, 0.0, None, ALU.min))
                    step.link(dve.memset(one_row, 1.0))
                    step.link(dve.memset(zero_row, 0.0))
                if k < 3:
                    evac2(k)
                if k == 3:
                    lo(u + 1, (u + 1) % 2)
                    dve.wait_ge(sm("softplus"), 1)
                    step.link(tt(f_row2, f_row2, lf_row, ALU.subtract))
                    step.link(dve.tensor_tensor_scan(b_row, one_row, f_row2, 0.0, ALU.mult, ALU.add))
                    step.link(tt(i_row, i_row, b_row, ALU.subtract))
                    step.link(dve.tensor_tensor_scan(m_row, i_row, zero_row, 0.0, ALU.max, ALU.add))
                    step.link(tt(bm_row, b_row, m_row, ALU.add))
                    step.link(ts(nm_row, m_row, -1.0, None, ALU.mult))
                    dve.sem_inc(sm("gate_rows"), 1)
                    evac2(k)
            dve.wait_ge(sm("a_turned"), 1)
            cp(a_col, T[:, 0, 0:16])
            cp(nlam, T[:, 1, 0:1]).then_inc(sm("a_cols"), 1)
            dve.wait_ge(sm("a_cols"), 1)

            for h in range(4):
                k = 5 + 2 * h
                dve.wait_ge(sm("nm_ready"), h + 1)
                tt(nmd.rearrange("p (b c) -> p b c", b=NB), nm.rearrange("p (b c) -> p b c", b=NB),
                   mask_s.unsqueeze(1).to_broadcast([P, NB, P]), ALU.add).then_inc(sm("nmd_ready"), 1)
                evac2(k - 1)
                lo(U_IN2 + k + 1, (k + 1) % 2)
                dve.wait_ge(sm("dm_ready"), h + 1)
                dve.wait_ge(sm("mscores"), h + 1)
                for b in range(NB):
                    bank, at = S_BANK[b]
                    ins = stt(pm[b], T[:, bank, at:at + TRI[b]], DQK ** -0.5, pm[b], ALU.mult, ALU.mult)
                ins.then_inc(sm("pm_ready"), 1)
                evac2(k)
                lo(U_IN2 + k + 2, k % 2)
                dve.wait_ge(sm("msq_ready"), h + 1)
                step.link(stt(em2[:, :], em2[:, :], 1e24, nmd, ALU.min, ALU.max))
                dve.wait_ge(sm("mvar_done"), h + 1)
                stt(em2[:, :], em2[:, :], HEAD * EPS, T[:, 2], ALU.mult, ALU.add).then_inc(sm("mvar_ready"), 1)
                dve.wait_ge(sm("m_rstd"), h + 1)
                tt(tmp[:, 0], T[:, 0], em2[:, :], ALU.mult).then_inc(sm("num_read"), 1)
                dve.wait_ge(sm("num_read"), h + 1)
                dve.wait_ge(sm("mo_ready"), 1 + h // 2)
                stt(tmp[:, 0], tmp[:, 0], col2[:, 53 + h:54 + h], mo[:, h], ALU.mult, ALU.mult).then_inc(sm("m_out"), 1)
                dve.wait_ge(sm("m_out"), h + 1)
                split_lo(X_O + h, ga_lo[:, 4 + h], tmp[:, 0], ga_hi[:, 4 + h])
            evac2(12)

            def row_max(h, c):
                bank = T if c == 0 else G
                dve.wait_ge(sm("dscores"), 2 * h + c + 1)
                for b in range(NB):
                    q, at = Q_BANK[b]
                    d = bank[:, q, at + P * b:at + P * b + P]
                    ins = tt(d, d, mask_q, ALU.add)
                step.link(ins)
                for b in range(NB):
                    q, at = Q_BANK[b]
                    ins = dve.tensor_reduce(row_top[:, b:b + 1], bank[:, q, at:at + P * (b + 1)], AX.X, ALU.max)
                step.link(ins)
                ts(nmax[h % 2][:, 4 * c:4 * c + 4], row_top, -(DQK ** -0.5), None, ALU.mult).then_inc(sm("nmax"), 1)
                dve.wait_ge(sm("nmax"), 2 * h + c + 1)

            def difference(h):
                p0, p1 = pr[h % 2]
                z = sums[h % 2]
                dve.wait_ge(sm("p_ready"), 2 * h + 1)
                step.link(dve.reciprocal(z[:, 0:4], z[:, 0:4]))
                for b in range(NB):
                    r = slice(QAT[b], QAT[b] + P * (b + 1))
                    ins = ts(p0[:, r], p0[:, r], z[:, b:b + 1], None, ALU.mult)
                step.link(ins)
                dve.wait_ge(sm("p_ready"), 2 * h + 2)
                step.link(dve.reciprocal(z[:, 4:8], z[:, 4:8]))
                step.link(ts(z[:, 4:8], z[:, 4:8], nlam, None, ALU.mult))
                for b in range(NB):
                    r = slice(QAT[b], QAT[b] + P * (b + 1))
                    ins = stt(p0[:, r], p1[:, r], z[:, 4 + b:5 + b], p0[:, r], ALU.mult, ALU.add)
                ins.then_inc(sm("pd_ready"), 1)
                dve.wait_ge(sm("pd_ready"), h + 1)

            row_max(0, 0)
            row_max(0, 1)
            difference(0)
            for h in range(4):
                if h < 3:
                    row_max(h + 1, 0)
                    row_max(h + 1, 1)
                    difference(h + 1)
                else:
                    lo(U_OUT2 + 1, (U_OUT2 + 1) % 2)
                dve.wait_ge(sm("d_rstd"), h + 1)
                tt(tmp[:, h % 2], pv_bank(h), drs, ALU.mult).then_inc(sm("d_out"), 1)
                dve.wait_ge(sm("d_out"), h + 1)
                dve.wait_ge(sm("x_hi"), X_O + 4 + h + 1)
                stt(ga_lo[:, h], tmp[:, h % 2], dgain[:, 0:1], ga_hi[:, h].bitcast(F32), ALU.mult, ALU.subtract)\
                    .then_inc(sm("x_split"), 1)
                dve.wait_ge(sm("x_split"), X_O + 4 + h + 1)

            for j in range(4):
                u = U_OUT2 + j
                if j >= 1:
                    lo(u + 1, (u + 1) % 2)
                dve.wait_ge(sm("unit_done"), done(u))
                cp(acc[:, 2 * j:2 * j + 2], ps(u % 2)).then_inc(sm("evac"), 1)
            dve.wait_ge(sm("rstd_ready"), 4)
            dve.wait_ge(sm("x_block1"), 4)
            for j in range(5):
                if j < 3:
                    step.link(tt(tmp[:, :, :], acc[:, 2 * j:2 * j + 2], bc2(rstd[:, :]), ALU.mult))
                    for n in range(2):
                        c = 2 * j + n
                        ins = stt(X[:, c], tmp[:, n], col2[:, 8 + c:9 + c], X[:, c], ALU.mult, ALU.add)
                    ins.then_inc(sm("x_new"), 1)
                    dve.wait_ge(sm("x_new"), j + 1)
                if j == 4:
                    dve.wait_ge(sm("x_new_last"), 1)
                if j >= 1:
                    scaled_lo(X_H4 + j - 1, h2_lo, h2_hi, col2[:, 16:24], j - 1)

            def mlp_up(u, xk):
                for m in range(4):
                    p = (U_MLP + m) % 2
                    lo(u + m + 1, 1 - p)
                    dve.wait_ge(sm("unit_done"), done(u + m))
                    dve.wait_ge(sm("rstd_ready"), 5)
                    stt(tmp[:, :, :], ps(p), 0.0, bc2(rstd[:, :]), ALU.max, ALU.mult).then_inc(sm("evac"), 1)
                    dve.wait_ge(sm("evac"), done(u + m))
                    step.link(tt(gate, tmp[:, :, :], tmp[:, :, :], ALU.mult))
                    split_lo(xk + m, ga_lo[:, 2 * m:2 * m + 2], gate, ga_hi[:, 2 * m:2 * m + 2])

            def mlp_down(u, m, first=False):
                dve.wait_ge(sm("unit_done"), done(u))
                if first:
                    cp(acc[:, 2 * m:2 * m + 2], ps((U_MLP + m) % 2)).then_inc(sm("evac"), 1)
                    return
                tt(acc[:, 2 * m:2 * m + 2], ps((U_MLP + m) % 2), acc[:, 2 * m:2 * m + 2], ALU.add)\
                    .then_inc(sm("evac"), 1)

            def mlp(u, xk, first=False):
                mlp_up(u, xk)
                for m in range(4):
                    lo(u + 5 + m, (U_MLP + m + 1) % 2)
                    mlp_down(u + 4 + m, m, first)

            mlp(U_MLP, X_HID2, True)
            with step.loop(1, 3, 4) as g:
                mlp(U_MLP + 8 * g, X_HID2 + 4 * g)
            mlp_up(U_MLP + 24, X_HID2 + 12)
            for m in range(4):
                u = U_MLP + 28 + m
                if u + 1 < U_END:
                    lo(u + 1, (u + 1) % 2)
                mlp_down(u, m)
            dve.wait_ge(sm("rstd_ready"), 6)
            for j in range(3):
                t = acc[:, 2 * j:2 * j + 2]
                step.link(tt(t, t, bc2(rstd[:, :]), ALU.mult))
                for n in range(2):
                    c = 2 * j + n
                    ins = stt(t[:, n], t[:, n], col2[:, 24 + c:25 + c], X[:, c], ALU.mult, ALU.add)
                ins.then_inc(sm("result"), 1)

        @block.tensor
        def _(pe):
            mm = pe.matmul

            def begin(u, first=False):
                pe.wait_ge(sm("lo_split"), done(u))
                pe.wait_ge(sm("evac"), free(u))

            def unit(u, p, xh, xl, kc=KC, xk=None, order=None):
                begin(u)
                order = order or list(range(kc))
                for a, t in enumerate(order):
                    if xk is not None and a % 2 == 0:
                        pe.wait_ge(sm("x_split"), xk + a // 2 + 1)
                    for n in range(2):
                        c = slice(n * P, (n + 1) * P)
                        for q, (wt, x) in enumerate(((w_hi, xh), (w_hi, xl), (w_lo, xh))):
                            ins = mm(G[:, 2 * p + n], wt[:, p, t, c], x[:, t], start=(a == 0 and q == 0),
                                     stop=(a == kc - 1 and q == 2))
                ins.then_inc(sm("unit_done"), 1)

            def value_block(p, b, xh, xl):
                o = G[:, 2 * p + b // 2, (b % 2) * UC:(b % 2 + 1) * UC]
                for t in range(KC):
                    for q, (x, wt) in enumerate(((xh, w_hi), (xl, w_hi), (xh, w_lo))):
                        ins = mm(o, x[:, t, b * P:(b + 1) * P], wt[:, p, t, :], start=(t == 0 and q == 0),
                                 stop=(t == KC - 1 and q == 2))
                return ins

            def stats(k, bank, first, last):
                pe.wait_ge(sm("sq_ready"), k + 1)
                for n in range(2):
                    ins = mm(T[:, bank], ones[:, :], sq_buf(k)[:, n], start=(first and n == 0), stop=(last and n == 1),
                             skip_group_check=True)
                ins.then_inc(sm("sq_used"), 1)

            def chunk_sum(n_sq, bank, o):
                pe.wait_ge(sm("sq_used"), n_sq)
                mm(T[:, bank], ones[:, :], sq_sum[o], start=True, stop=False, skip_group_check=True)

            def causal_sum(o, vals, at, probs):
                for b in range(NB):
                    ins = mm(o[:, P * b:S], vals[:, b, at:at + P], probs[b],
                             start=(b == 0), stop=(b == NB - 1), skip_group_check=True)
                return ins

            def mod_cols(third):
                for k in range(16):
                    ins = mm(T[:, 0, k:k + 1], ada_sum[:, k * P:(k + 1) * P], ones[:, 0:1], start=True, stop=True)
                ins.then_inc(sm("mod_done"), 1)

            pe.wait_ge(sm("par_in"), 16 * (len(PAR1) + 1))
            pe.transpose(T[:, 0, 0:N1], prow1, ident[0:N1, 0:N1]).then_inc(sm("turned1"), 1)
            pe.wait_ge(sm("x_in"), 16)
            for t in range(KC):
                if t >= 4:
                    pe.wait_ge(sm("x_ready"), t - 3)
                for b in range(NB):
                    ins = pe.transpose(G[:, t % 4, b * P:(b + 1) * P], xin[:, b, t * P:(t + 1) * P], ident)
                ins.then_inc(sm("x_t"), 1)
            pe.wait_ge(sm("pads"), 1)
            for j in range(4):
                stats(j, 1, j == 0, j == 3)
            pe.wait_ge(sm("x_ready"), 8)
            pe.wait_ge(sm("par2_in"), 16 * (len(PAR2) + 6))
            pe.transpose(T[:, 2, 0:N2], prow2, ident[0:N2, 0:N2]).then_inc(sm("turned2"), 1)
            pe.wait_ge(sm("ada_used"), done(7))
            pe.wait_ge(sm("col2_ready"), 1)
            pe.wait_ge(sm("rstd_ready"), 1)
            for j in range(4):
                for k in (2 * j, 2 * j + 1, 8 + 2 * j, 9 + 2 * j):
                    ins = mm(T[:, j, k:k + 1], ada_sum[:, k * P:(k + 1) * P], ones[:, 0:1], start=True, stop=True)
                ins.then_inc(sm("mod1_part"), 1)

            with pe.Fori(0, 2) as i:
                for k in range(6):
                    unit(U_CONV + 6 * i + k, k % 2, h_hi, h_lo, xk=X_H1 if k == 0 else None)
            pe.wait_ge(sm("ada_used"), done(15))
            mod_cols(1)
            with pe.Fori(0, 4) as i:
                unit(U_COUT + 2 * i, 0, h_hi, h_lo)
                pe.wait_ge(sm("x_split"), X_CV + 4)
                unit(U_COUT + 2 * i + 1, 1, ga_hi, ga_lo)
            pe.wait_ge(sm("ada_used"), done(23))
            mod_cols(2)
            with pe.Fori(0, 4) as i:
                u = U_RET + 4 * i
                unit(u, 0, h_hi, h_lo)
                unit(u + 1, 1, h_hi, h_lo)

                def scores(h):
                    for b in range(NB):
                        bank, at = S_BANK[b]
                        ins = mm(T[:, bank, at:at + TRI[b]], kk[:, h, b * P:(b + 1) * P], qq[:, h, b * P:S],
                                 start=True, stop=True)
                    ins.then_inc(sm("scores"), 1)

                begin(u + 2)
                for b in range(3):
                    value_block(0, b, h_hi, h_lo)
                pe.wait_ge(sm("rotated"), 2 * i + 2)
                scores(0)
                value_block(0, 3, h_hi, h_lo).then_inc(sm("unit_done"), 1)
                pe.wait_ge(sm("scores_used"), 2 * i + 3)
                scores(1)

                def g_tile(n):
                    for t in range(KC):
                        for q, (wt, x) in enumerate(((w_hi, h_hi), (w_hi, h_lo), (w_lo, h_hi))):
                            ins = mm(G[:, 2 + n], wt[:, 1, t, n * P:(n + 1) * P], x[:, t], start=(t == 0 and q == 0),
                                     stop=(t == KC - 1 and q == 2))
                    return ins

                begin(u + 3)
                g_tile(0)
                pe.wait_ge(sm("scores_used"), 2 * i + 4)
                pe.wait_ge(sm("evac"), done(u + 2))
                for h in range(2):
                    causal_sum(T[:, 2 + h], vv, h * P, pp_blocks[h]).then_inc(sm("pv_done"), 1)
                g_tile(1).then_inc(sm("unit_done"), 1)
                pe.wait_ge(sm("ysq_ready"), i + 1)
                for h in range(2):
                    ins = mm(T[:, h], ones[:, :], sqp[:, h], start=True, stop=True)
                ins.then_inc(sm("var_done"), 1)
            with pe.Fori(0, 2) as i:
                for m in range(2):
                    unit(U_GA + 2 * i + m, m, h_hi, h_lo)
            pe.wait_ge(sm("x_split"), X_RET + 4)
            with pe.Fori(0, 2) as i:
                for m in range(2):
                    unit(U_ROUT + 2 * i + m, m, ga_hi, ga_lo)
            for j in range(4):
                u = U_MIX + j
                unit(u, u % 2, h_hi, h_lo, xk=X_MRG if j == 0 else None)
            chunk_sum(7, 0, 1)
            stats(7, 0, False, True)

            def ffn(u, pairs):
                with pe.Fori(0, pairs) as i:
                    unit(u + 2 * i, 0, h_hi, h_lo, xk=X_H2)
                    unit(u + 2 * i + 1, 1, h_hi, h_lo)

            with pe.Fori(0, 2) as g:
                u = U_FFN + 12 * g
                ffn(u, 4)
                for m in range(4):
                    unit(u + 8 + m, m % 2, ga_hi, ga_lo, xk=X_HID + 4 * g if m == 0 else None)
            ffn(U_FFN + 24, 3)
            for j in range(4):
                u = U_FFN + 30 + j
                unit(u, u % 2, ga_hi, ga_lo, kc=6, xk=X_HID + 8 if j == 0 else None)

            def part(k, n):
                u = U_IN2 + k
                p = u % 2
                if n == 0:
                    begin(u)
                if IN2[k][1] == "v":
                    for b in (2 * n, 2 * n + 1):
                        ins = value_block(p, b, h_hi, h_lo)
                else:
                    for t in range(KC):
                        if k == 0 and t % 2 == 0:
                            pe.wait_ge(sm("x_split"), X_H3 + t // 2 + 1)
                        for q, (wt, x) in enumerate(((w_hi, h_hi), (w_hi, h_lo), (w_lo, h_hi))):
                            ins = mm(G[:, 2 * p + n], wt[:, p, t, n * P:(n + 1) * P], x[:, t], start=(t == 0 and q == 0),
                                     stop=(t == KC - 1 and q == 2))
                if n == 1 or IN2[k] == "gates":
                    ins.then_inc(sm("unit_done"), 1)

            part(0, 0)
            part(0, 1)
            chunk_sum(14, 0, 0)
            chunk_sum(14, 1, 1)
            stats(14, 0, False, True)
            stats(15, 1, False, True)
            part(1, 0)
            part(1, 1)
            part(2, 0)
            pe.wait_ge(sm("r12_ready"), 1)
            for b in range(NB):
                ins = mm(T[:, 2, b:b + 1], rstd[0:1, b * P:(b + 1) * P], ones[0:1, 0:1], start=True, stop=True)
            ins.then_inc(sm("r12_turned"), 1)
            part(3, 0)
            part(3, 1)
            part(4, 0)
            pe.wait_ge(sm("gate_rows"), 1)
            for b in range(NB):
                mm(T[:, 0, 4 * b:4 * b + 4], i_row[:, b * P:(b + 1) * P], ident[0:4, 0:4], start=True, stop=True)
            pe.wait_ge(sm("lam_ready"), 1)
            mm(T[:, 1, 0:1], ones[0:1, :], lam_row[:, 5:6], start=True, stop=True).then_inc(sm("a_turned"), 1)
            part(4, 1)
            pe.wait_ge(sm("a_cols"), 1)
            pe.wait_ge(sm("mqk_ready"), 2)
            for h in range(4):
                k = 5 + 2 * h
                if h >= 1:
                    pe.wait_ge(sm("num_read"), h)
                r = slice(DQK * (h % 2), DQK * (h % 2) + DQK)
                mm(T[:, 3], sel(h), nm_row, start=True, stop=True).then_inc(sm("m_bcast"), 1)
                for b in range(NB):
                    bank, at = S_BANK[b]
                    ins = mm(T[:, bank, at:at + TRI[b]], mqk[1][r, h // 2, b * P:(b + 1) * P],
                             mqk[0][r, h // 2, b * P:S], start=True, stop=True)
                ins.then_inc(sm("mscores"), 1)
                part(k, 0)
                part(k, 1)
                if h == 0:
                    pe.wait_ge(sm("evac"), done(U_IN2 + 4))
                pe.wait_ge(sm("pm_ready"), h + 1)
                mm(T[:, 3], sel(h), bm_row, start=True, stop=True)
                causal_sum(T[:, 0], vm, h * P, pm)
                for b in range(NB):
                    ins = mm(T[:, 1, P * b:S], ones[:, :], pm[b], start=(b == 0), stop=(b == NB - 1),
                             skip_group_check=True)
                ins.then_inc(sm("num_done"), 1)
                part(k + 1, 0)
                pe.wait_ge(sm("msq_ready"), h + 1)
                mm(T[:, 2], ones[:, :], nm, start=True, stop=True).then_inc(sm("mvar_done"), 1)
                part(k + 1, 1)

            def dscores(h, c):
                bank = T if c == 0 else G
                r = slice(DQK * c, DQK * c + DQK)
                for b in range(NB):
                    q, at = Q_BANK[b]
                    ins = mm(bank[:, q, at:at + P * (b + 1)], q2[r, h, b * P:(b + 1) * P], k2[r, h, 0:P * (b + 1)],
                             start=True, stop=True)
                ins.then_inc(sm("dscores"), 1)

            def turn(h, blocks):
                for kb in blocks:
                    for b in range(kb, NB):
                        ins = pe.transpose(turned(h, kb)[:, (b - kb) * P:(b - kb + 1) * P],
                                           pr[h % 2][0][:, QAT[b] + kb * P:QAT[b] + (kb + 1) * P], ident)
                ins.then_inc(sm("p_turned"), 1)

            def d_values(h):
                causal_sum(pv_bank(h), vd, h * P, [pt[:, TRI_AT[b]:TRI_AT[b] + TRI[b]] for b in range(NB)])\
                    .then_inc(sm("dpv_done"), 1)

            def d_norm(h):
                pe.wait_ge(sm("dsq_ready"), h + 1)
                mm(var_bank(h), ones[:, :], dsq, start=True, stop=True).then_inc(sm("dvar_done"), 1)

            pe.wait_ge(sm("rotated2"), 4)
            pe.wait_ge(sm("num_read"), 4)
            dscores(0, 0)
            pe.wait_ge(sm("evac"), done(U_IN2 + 12))
            dscores(0, 1)
            pe.wait_ge(sm("p_ready"), 1)
            dscores(1, 0)
            for h in range(3):
                pe.wait_ge(sm("pd_ready"), h + 1)
                if h >= 1:
                    pe.wait_ge(sm("d_out"), h)
                turn(h, (0, 1, 3))
                dscores(h + 1, 1)
                pe.wait_ge(sm("pt_ready"), 2 * h + 1)
                turn(h, (2,))
                pe.wait_ge(sm("pt_ready"), 2 * h + 2)
                d_values(h)
                d_norm(h)
                if h < 2:
                    pe.wait_ge(sm("p_ready"), 2 * h + 3)
                    dscores(h + 2, 0)

            def out_chunks(u, first, chunks):
                p = u % 2
                for a, t in enumerate(chunks):
                    for n in range(2):
                        for q, (wt, x) in enumerate(((w_hi, ga_hi), (w_hi, ga_lo), (w_lo, ga_hi))):
                            ins = mm(G[:, 2 * p + n], wt[:, p, t, n * P:(n + 1) * P], x[:, t],
                                     start=(first and a == 0 and q == 0), stop=(chunks[-1] == 3 and t == 3 and q == 2),
                                     skip_group_check=True)
                return ins

            begin(U_OUT2)
            pe.wait_ge(sm("p_ready"), 8)
            pe.wait_ge(sm("d_out"), 3)
            pe.wait_ge(sm("x_split"), X_O + 4)
            out_chunks(U_OUT2, True, (4, 5, 6, 7))
            pe.wait_ge(sm("pd_ready"), 4)
            turn(3, (0, 1, 3))
            turn(3, (2,))
            pe.wait_ge(sm("x_split"), X_O + 6)
            out_chunks(U_OUT2, False, (0, 1))
            pe.wait_ge(sm("pt_ready"), 8)
            d_values(3)
            pe.wait_ge(sm("x_split"), X_O + 7)
            out_chunks(U_OUT2, False, (2,))
            d_norm(3)
            begin(U_OUT2 + 1)
            out_chunks(U_OUT2 + 1, True, (4, 5, 6, 7))
            pe.wait_ge(sm("x_split"), X_O + 8)
            out_chunks(U_OUT2, False, (3,)).then_inc(sm("unit_done"), 1)
            out_chunks(U_OUT2 + 1, False, (0, 1, 2, 3)).then_inc(sm("unit_done"), 1)
            for j in range(2, 4):
                unit(U_OUT2 + j, (U_OUT2 + j) % 2, ga_hi, ga_lo)
            chunk_sum(19, 0, 1)
            stats(19, 0, False, True)

            def mlp_group(u, first=False):
                for m in range(4):
                    unit(u + m, (U_MLP + m) % 2, h2_hi, h2_lo, xk=X_H4 if first and m == 0 else None)
                    if first and m == 0:
                        chunk_sum(23, 1, 1)
                        stats(23, 1, False, True)

            def mlp(u, xk, first=False):
                mlp_group(u, first)
                for m in range(4):
                    unit(u + 4 + m, (U_MLP + m) % 2, ga_hi, ga_lo, xk=xk if m == 0 else None)

            mlp(U_MLP, X_HID2, True)
            with pe.Fori(1, 3) as g:
                mlp(U_MLP + 8 * g, X_HID2 + 4 * g)
            mlp_group(U_MLP + 24)
            for j in range(4):
                u = U_MLP + 28 + j
                unit(u, u % 2, ga_hi, ga_lo, xk=X_HID2 + 12 if j == 0 else None)
            chunk_sum(27, 0, 1)
            stats(27, 0, False, True)
            pe.wait_ge(sm("evac"), done(U_END - 1))
            for j in range(4):
                if j < 3:
                    pe.wait_ge(sm("result"), j + 1)
                else:
                    pe.wait_ge(sm("result_last"), 1)
                if j >= 2:
                    pe.wait_ge(sm("out_ready"), j - 1)
                for b in range(NB):
                    for n in range(2):
                        ins = pe.transpose(G[:, 2 * (j % 2) + b // 2, (b % 2) * UC + n * P:(b % 2) * UC + (n + 1) * P],
                                           acc[:, 2 * j + n, b * P:(b + 1) * P], ident)
                ins.then_inc(sm("out_turned"), 1)


_INS = ["x", "c", "positions", "ada_w", "ada_b", "norm_mix_g", "w_in", "conv_w", "ret_w_out", "conv_w_out",
        "mix_w_out", "norm_ffn_g", "ffn_w_gate", "ffn_w_up", "ffn_w_down", "final_norm_g", "norm_mix_pre_2",
        "w_in_2", "conv_w_2", "conv_b_2", "b_igate_2", "b_fgate_2", "lambda_q1_2", "lambda_k1_2",
        "lambda_q2_2", "lambda_k2_2", "diff_norm_2", "mlstm_norm_2", "w_out_2", "norm_mix_post_2",
        "norm_mlp_pre_2", "w_up_2", "w_down_2", "norm_mlp_post_2"]


def constants():
    con = np.zeros((P, C_ALL), np.float32)
    p = np.arange(P)
    con[:, C_ID:C_ID + P] = np.eye(P)
    con[:, C_MS:C_MS + P] = np.where(p[:, None] <= p[None, :], 0.0, -BIG)
    con[:, C_MQ:C_MQ + P] = np.where(p[None, :] <= p[:, None], 0.0, -BIG)
    half = DQK // 2
    inv = (10000.0 ** (-2.0 * (p % half) / DQK)).astype(np.float32)
    ang = (np.arange(S, dtype=np.float32)[None, :] * inv[:, None]).astype(np.float64)
    con[:, C_COS2:C_COS2 + S] = np.cos(ang)
    con[:, C_SIN2:C_SIN2 + S] = np.sin(ang) * np.where(p % DQK < half, -1.0, 1.0)[:, None]
    con[:, C_INVF] = 10000.0 ** (-2.0 * (p % (HEAD // 2)) / HEAD)
    far = np.arange(S)[None, :] - p[:, None]
    decay = np.zeros((8, P, S), np.float32)
    for h in range(8):
        gamma = 1.0 - 2.0 ** (-5.0 - h)
        decay[h] = np.where(far >= 0, gamma ** np.maximum(far, 0), 0.0) * HEAD ** -0.5
    return con, decay


def kernel(**inputs):
    import concourse.bacc as _bacc
    from concourse.bass_utils import run_bass_kernel_spmd as _run

    nc = _bacc.Bacc("TRN2", target_bir_lowering=False, num_devices=1)
    data = {name: np.ascontiguousarray(inputs[name]) for name in _INS}
    data["consts"], data["decay"] = constants()
    arrays, args = {}, {}
    for name, a in data.items():
        arrays[f"in_{name}_dram"] = a
        args[name] = nc.dram_tensor(f"in_{name}_dram", a.shape, mybir.dt.from_np(a.dtype), kind="ExternalInput").ap()
    out = nc.dram_tensor("out_0_dram", (1, S, D), F32, kind="ExternalOutput").ap()
    program(nc, args, out)
    r = _run(nc, [arrays], core_ids=[0])
    return r.results[0]["out_0_dram"]
```
